# Optimizing a Trainium2 kernel written in Bass

```python
import jax, jax.numpy as jnp
from jax import lax
import numpy as np

D_MODEL = 1024
BATCH = 1
SEQ = 256
DEPTH = 2

N_META = 16
N_A_LAYERS = DEPTH // 2
N_B_LAYERS = DEPTH - N_A_LAYERS
N_HEADS = 8
HEAD_DIM = D_MODEL // N_HEADS
N_KV_HEADS = 2
GROUP = N_HEADS // N_KV_HEADS
ROPE_THETA = 500000.0
IDX_HEADS = 4
IDX_DIM = 64
INDEX_TOPK = 256
Q_BLOCK = 128
PEER_HEADS = 8
PEER_QUERY_DIM = 256
PEER_HALF = PEER_QUERY_DIM // 2
N_KEYS = 128
N_EXPERTS = N_KEYS * N_KEYS
PEER_TOPK = 16
PEER_CHUNK = 128
RMS_EPS = 1e-6

A_Q = N_HEADS * HEAD_DIM
A_K = N_KV_HEADS * HEAD_DIM
A_V = N_KV_HEADS * HEAD_DIM
A_QI = IDX_HEADS * IDX_DIM
A_KI = IDX_DIM
A_WI = IDX_HEADS
A_COLS = A_Q + A_K + A_V + A_QI + A_KI + A_WI
A_SPLITS = [A_Q, A_Q + A_K, A_Q + A_K + A_V, A_Q + A_K + A_V + A_QI, A_Q + A_K + A_V + A_QI + A_KI]

kernel_name = "yoco_dsa_stickbreak_peer_meta"

def rms_norm(x, gain):
    xf = x.astype(jnp.float32)
    y = xf * lax.rsqrt(jnp.mean(xf * xf, axis=-1, keepdims=True) + RMS_EPS)
    return (y * gain.astype(jnp.float32)).astype(x.dtype)

def partial_rope(x, pos):
    d = x.shape[-1]
    r = d // 4
    half = r // 2
    inv = ROPE_THETA ** (-jnp.arange(half, dtype=jnp.float32) * 2.0 / r)
    ang = pos[:, None] * inv[None, :]
    cos = jnp.cos(ang)[None, :, None, :]
    sin = jnp.sin(ang)[None, :, None, :]
    xf = x.astype(jnp.float32)
    x1 = xf[..., :half]
    x2 = xf[..., half:r]
    out = jnp.concatenate([x1 * cos - x2 * sin, x2 * cos + x1 * sin, xf[..., r:]], axis=-1)
    return out.astype(x.dtype)

def to_blocks(a):
    b, t = a.shape[:2]
    a = a.reshape((b, t // Q_BLOCK, Q_BLOCK) + a.shape[2:])
    return jnp.moveaxis(a, 1, 0)

def from_blocks(a):
    a = jnp.moveaxis(a, 0, 1)
    return a.reshape((a.shape[0], a.shape[1] * a.shape[2]) + a.shape[3:])

def dsa_attention(hn, w_in, q_gain, k_gain, w_o, pos, topk):
    b, t, _ = hn.shape
    proj = hn @ w_in
    q, k, v, qi, ki, wi = jnp.split(proj, A_SPLITS, axis=-1)
    q = partial_rope(rms_norm(q.reshape(b, t, N_HEADS, HEAD_DIM), q_gain), pos)
    k = partial_rope(rms_norm(k.reshape(b, t, N_KV_HEADS, HEAD_DIM), k_gain), pos)
    v = v.reshape(b, t, N_KV_HEADS, HEAD_DIM)
    qi = partial_rope(qi.reshape(b, t, IDX_HEADS, IDX_DIM), pos) * (IDX_DIM ** -0.5)
    ki = partial_rope(ki.reshape(b, t, 1, IDX_DIM), pos)[:, :, 0]
    wi = wi * (IDX_HEADS ** -0.5)
    key_pos = jnp.arange(t)
    gather = jax.vmap(lambda a, i: a[i])

    def block(args):
        qb, qib, wib, t0 = args
        qpos = t0 + jnp.arange(Q_BLOCK)
        causal = key_pos[None, :] <= qpos[:, None]
        score = jnp.einsum('bqhd,bsd->bqhs', qib.astype(jnp.float32), ki.astype(jnp.float32))
        score = jnp.einsum('bqhs,bqh->bqs', jax.nn.relu(score), wib.astype(jnp.float32))
        score = jnp.where(causal[None], score, -jnp.inf)
        _, sel = lax.top_k(score, topk)
        valid = sel <= qpos[None, :, None]
        k_sel = gather(k, sel)
        v_sel = gather(v, sel)
        qg = qb.reshape(b, Q_BLOCK, N_KV_HEADS, GROUP, HEAD_DIM)
        logits = jnp.einsum('bqhgd,bqnhd->bqhgn', qg, k_sel).astype(jnp.float32) * (HEAD_DIM ** -0.5)
        logits = jnp.where(valid[:, :, None, None, :], logits, -jnp.inf)
        p = jax.nn.softmax(logits, axis=-1).astype(v.dtype)
        o = jnp.einsum('bqhgn,bqnhd->bqhgd', p, v_sel)
        return o.reshape(b, Q_BLOCK, N_HEADS * HEAD_DIM)

    starts = jnp.arange(t // Q_BLOCK) * Q_BLOCK
    o = lax.map(block, (to_blocks(q), to_blocks(qi), to_blocks(wi), starts))
    return from_blocks(o) @ w_o

def stick_breaking_attention(hn, w_q, w_o, k, v):
    b, t, _ = hn.shape
    q = (hn @ w_q).reshape(b, t, N_KV_HEADS, GROUP, HEAD_DIM)
    key_pos = jnp.arange(t)

    def block(args):
        qb, t0 = args
        qpos = t0 + jnp.arange(Q_BLOCK)
        causal = key_pos[None, :] < qpos[:, None]
        z = jnp.einsum('bqhgd,bshd->bhgqs', qb, k).astype(jnp.float32) * (HEAD_DIM ** -0.5)
        log_keep = jnp.where(causal, jax.nn.log_sigmoid(-z), 0.0)
        between = lax.cumsum(log_keep, axis=4, reverse=True) - log_keep
        a = jnp.where(causal, jnp.exp(jax.nn.log_sigmoid(z) + between), 0.0).astype(v.dtype)
        o = jnp.einsum('bhgqs,bshd->bqhgd', a, v)
        return o.reshape(b, Q_BLOCK, N_HEADS * HEAD_DIM)

    starts = jnp.arange(t // Q_BLOCK) * Q_BLOCK
    o = lax.map(block, (to_blocks(q), starts))
    return from_blocks(o) @ w_o

def peer_ffn(hn, w_q, subkeys, u, v):
    b, t, d = hn.shape
    n = b * t
    xt = hn.reshape(n, d)
    q = (xt @ w_q).reshape(n, PEER_HEADS, 2, PEER_HALF)
    s = jnp.einsum('nhcd,ckd->nhck', q, subkeys).astype(jnp.float32)
    s_top, i_top = lax.top_k(s, PEER_TOPK)
    cand = s_top[:, :, 0, :, None] + s_top[:, :, 1, None, :]
    cand_id = i_top[:, :, 0, :, None] * N_KEYS + i_top[:, :, 1, None, :]
    best, pick = lax.top_k(cand.reshape(n, PEER_HEADS, PEER_TOPK * PEER_TOPK), PEER_TOPK)
    ids = jnp.take_along_axis(cand_id.reshape(n, PEER_HEADS, PEER_TOPK * PEER_TOPK), pick, axis=-1)
    g = jax.nn.softmax(best, axis=-1).astype(hn.dtype)
    n_chunks = n // PEER_CHUNK

    def chunk(args):
        xc, ic, gc = args
        u_sel = u[ic]
        v_sel = v[ic]
        act = jax.nn.gelu(jnp.einsum('cd,ced->ce', xc, u_sel), approximate=False) * gc
        return jnp.einsum('ce,ced->cd', act, v_sel)

    out = lax.map(chunk, (xt.reshape(n_chunks, PEER_CHUNK, d),
                          ids.reshape(n_chunks, PEER_CHUNK, PEER_HEADS * PEER_TOPK),
                          g.reshape(n_chunks, PEER_CHUNK, PEER_HEADS * PEER_TOPK)))
    return out.reshape(b, t, d)

def setup_inputs(seed: int = 0) -> dict:
    key = jax.random.key(seed)
    ks = jax.random.split(key, 20)
    f32 = jnp.float32
    hd = N_HEADS * HEAD_DIM

    def nrm(k, shape, scale):
        return jax.random.normal(k, shape, f32) * scale

    def gain(k, shape):
        return 1.0 + 0.02 * jax.random.normal(k, shape, f32)

    return {
        "x": nrm(ks[0], (BATCH, SEQ, D_MODEL), 1.0),
        "meta_tokens": nrm(ks[1], (N_META, D_MODEL), 1.0),
        "a_norm": gain(ks[2], (N_A_LAYERS, D_MODEL)),
        "a_w_in": nrm(ks[3], (N_A_LAYERS, D_MODEL, A_COLS), D_MODEL ** -0.5),
        "a_q_norm": gain(ks[4], (N_A_LAYERS, HEAD_DIM)),
        "a_k_norm": gain(ks[5], (N_A_LAYERS, HEAD_DIM)),
        "a_w_o": nrm(ks[6], (N_A_LAYERS, hd, D_MODEL), hd ** -0.5),
        "kv_norm": gain(ks[7], (D_MODEL,)),
        "kv_w": nrm(ks[8], (D_MODEL, 2 * N_KV_HEADS * HEAD_DIM), D_MODEL ** -0.5),
        "b_norm": gain(ks[9], (N_B_LAYERS, D_MODEL)),
        "b_w_q": nrm(ks[10], (N_B_LAYERS, D_MODEL, hd), D_MODEL ** -0.5),
        "b_w_o": nrm(ks[11], (N_B_LAYERS, hd, D_MODEL), hd ** -0.5),
        "ffn_norm": gain(ks[12], (DEPTH, D_MODEL)),
        "peer_w_q": nrm(ks[13], (DEPTH, D_MODEL, PEER_HEADS * PEER_QUERY_DIM), D_MODEL ** -0.5),
        "peer_subkeys": nrm(ks[14], (DEPTH, 2, N_KEYS, PEER_HALF), PEER_HALF ** -0.5),
        "peer_u": nrm(ks[15], (DEPTH, N_EXPERTS, D_MODEL), D_MODEL ** -0.5),
        "peer_v": nrm(ks[16], (DEPTH, N_EXPERTS, D_MODEL), 0.1),
    }

def reference(x, meta_tokens, a_norm, a_w_in, a_q_norm, a_k_norm, a_w_o, kv_norm, kv_w,
              b_norm, b_w_q, b_w_o, ffn_norm, peer_w_q, peer_subkeys, peer_u, peer_v):
    b, s, d = x.shape
    t = s + N_META
    t_pad = -(-t // Q_BLOCK) * Q_BLOCK
    h = jnp.concatenate([jnp.broadcast_to(meta_tokens[None].astype(x.dtype), (b, N_META, d)), x], axis=1)
    h = jnp.pad(h, ((0, 0), (0, t_pad - t), (0, 0)))
    pos = jnp.arange(t_pad, dtype=jnp.float32)
    topk = min(INDEX_TOPK, s // 4)
    shared_k = None
    shared_v = None
    for layer in range(DEPTH):
        if layer < N_A_LAYERS:
            h = h + dsa_attention(rms_norm(h, a_norm[layer]), a_w_in[layer], a_q_norm[layer],
                                  a_k_norm[layer], a_w_o[layer], pos, topk)
        else:
            j = layer - N_A_LAYERS
            h = h + stick_breaking_attention(rms_norm(h, b_norm[j]), b_w_q[j], b_w_o[j], shared_k, shared_v)
        h = h + peer_ffn(rms_norm(h, ffn_norm[layer]), peer_w_q[layer], peer_subkeys[layer],
                         peer_u[layer], peer_v[layer])
        if layer == N_A_LAYERS - 1:
            kv = (rms_norm(h, kv_norm) @ kv_w).reshape(b, t_pad, 2 * N_KV_HEADS, HEAD_DIM)
            shared_k, shared_v = jnp.split(kv, 2, axis=2)
    return h[:, N_META:N_META + s]


_drawn_inputs = setup_inputs


def setup_inputs(seed=0):
    import zlib

    import numpy as np

    out = dict(_drawn_inputs(seed))
    spreads = {}
    factors = {'a_q_norm': 8.0, 'a_k_norm': 8.0, 'kv_norm': 4.544, 'b_norm': 8.0, 'ffn_norm': 5.525}
    for name, (base, spread) in spreads.items():
        noise = np.random.default_rng([zlib.crc32(name.encode()), seed]).standard_normal(out[name].shape)
        drawn = base * np.exp(spread * noise) if base else spread * noise
        out[name] = __import__('jax').numpy.asarray(drawn.astype(out[name].dtype))
    for name, factor in factors.items():
        out[name] = (out[name] * factor).astype(out[name].dtype)
    return out
```

```python
from contextlib import ExitStack

import concourse.bass as bass
from concourse import mybir

F32 = mybir.dt.float32
U32 = mybir.dt.uint32
ALU = mybir.AluOpType
ACT = mybir.ActivationFunctionType
AX = mybir.AxisListType

P = 128
D = 1024
KC = D // P
META = 16
TILES = 3
NT = [META, P, P]
OFF = [0, META, META + P]
T = META + 2 * P
KEYS = [META, META + P, T]
HEADS = 8
KV = 2
GROUP = HEADS // KV
IDX_HEADS = 4
TOPK = 64
A_COLS = 1860
EXPERTS = 16384
NKEYS = 128
SEL = 16
GT = 16
SCALE = 128.0 ** -0.5
IDX_SCALE = 1.0 / 16.0
EPS = 1e-6
NEG = -1.0e30
MASKED = -3.0e38
TAKEN = -3.4e38
TAKEN_BELOW = -3.2e38


class Chain:

    def __init__(self, eng, sem):
        self.eng, self.sem, self.n, self.off = eng, sem, 0, 0

    def do(self, ins):
        self.n += 1
        ins.then_inc(self.sem, 1)
        self.eng.wait_ge(self.sem, self.n + self.off)


def build(nc, x, meta, a_norm, a_w_in, a_q_norm, a_k_norm, a_w_o, kv_norm, kv_w, b_norm, b_w_q, b_w_o,
          ffn_norm, peer_w_q, peer_subkeys, peer_u, peer_v, rope, out):
    u_rows = peer_u.rearrange("l e d -> (l e) d")
    v_rows = peer_v.rearrange("l e d -> (l e) d")
    with ExitStack() as ctx:
        def sb(name, cols, dt=F32, rows=P):
            return ctx.enter_context(nc.sbuf_tensor(name, [rows, cols], dt))

        def sem(name):
            return ctx.enter_context(nc.semaphore(name))

        bank = ctx.enter_context(nc.psum_tensor("banks", [P, 8, 512], F32))

        arena = sb("arena", 28672)
        ring = arena[:, 0:16 * D].rearrange("p (k d) -> p k d", d=D)
        w_in = arena[:, 0:KC * A_COLS].rearrange("p (c n) -> p c n", n=A_COLS)
        W0 = KC * A_COLS
        a_wo = arena[:, W0:W0 + 8192].rearrange("p (h n) -> p h n", n=D)
        pq_at = [[W0 + 8192, 0, 4096, 8192], [8192, 12288, 16384, 20480]]
        pq = [[arena[:, a:a + 4096].rearrange("p (c n) -> p c n", n=512) for a in at] for at in pq_at]
        b_wq = arena[:, 16384:24576].rearrange("p (c n) -> p c n", n=D)
        kv_ws = arena[:, 24576:28672].rearrange("p (c n) -> p c n", n=512)
        b_wo = arena[:, 0:8192].rearrange("p (h n) -> p h n", n=D)

        hx_t = sb("residual", TILES * D)
        hx = hx_t[:, :].rearrange("p (i d) -> p i d", d=D)
        x1_t = sb("x_norm_T", KC * T)
        xT = x1_t[:, :].rearrange("p (c n) -> p c n", n=T)
        x2_t = sb("kv_norm_T", KC * T)
        xT2 = x2_t[:, :].rearrange("p (c n) -> p c n", n=T)
        qt_t = sb("queries_T", 2 * 17 * P)
        QT = qt_t[:, :].rearrange("p (c g m) -> p c g m", c=2, m=P)
        QTw = qt_t[:, :].rearrange("p (c g h t) -> p c g h t", c=2, h=HEADS, t=GT)
        PJ = qt_t[:, 0:1920].rearrange("p (b d) -> p b d", d=P)
        L = qt_t[:, 2048:2048 + GROUP * T].rearrange("p (h k) -> p h k", k=T)
        qTB = qt_t[:, 0:2048].rearrange("p (h n) -> p h n", n=2 * P)
        E4 = qt_t[:, 3136:3136 + GROUP * T].rearrange("p (h k) -> p h k", k=T)
        SC = qt_t[:, 3136:3136 + T]
        WK = qt_t[:, 3408:3408 + T]
        qT = x2_t[:, 0:D].rearrange("p (h n) -> p h n", n=P)
        R4 = x2_t[:, D:D + GROUP * T].rearrange("p (h k) -> p h k", k=T)
        C4 = x2_t[:, 0:GROUP * T].rearrange("p (h k) -> p h k", k=T)
        dg_t = sb("diagonals", 16 * P)
        DG = dg_t[:, :].rearrange("p (k m) -> p k m", m=P)
        TMP = dg_t[:, 0:1280]
        PT = dg_t[:, 0:3 * 512].rearrange("p (j m) -> p j m", m=512)
        XR = sb("x_rows", D)
        oT_t = sb("heads_T", D)
        oT = oT_t[:, :].rearrange("p (h n) -> p h n", n=P)
        grow = sb("ffn_gain_row", D)
        V_t = sb("values", TILES * 256)
        V = V_t[:, :].rearrange("p (i d) -> p i d", d=256)
        kT_t = sb("keys_T", KV * T)
        kT = kT_t[:, :].rearrange("p (g k) -> p g k", k=T)
        kiT = sb("index_keys_T", T)
        qiT_t = sb("index_queries_T", 2 * P)
        qiT = qiT_t[:, :].rearrange("p (a n) -> p a n", n=P)
        WI = sb("index_weights", IDX_HEADS)
        BIAS = sb("bias", T)
        rope_t = sb("rope", TILES * 48)
        RO = rope_t[:, :].rearrange("p (i c) -> p i c", c=48)
        qg = sb("q_gain", P)
        kg = sb("k_gain", P)
        g_rows = sb("gain_rows", P)
        gcol = sb("gain_columns", 40)
        sk_rows_t = sb("subkeys", 4 * P)
        sk_rows = sk_rows_t[:, :].rearrange("p (m d) -> p m d", d=P)
        skT_t = sb("subkeys_T", 4 * P)
        skT = skT_t[:, :].rearrange("p (m k) -> p m k", k=P)
        ident = sb("ident", P)
        zeros = sb("zeros", P)
        ones = sb("ones", T)
        iota16 = sb("iota16", SEL)
        spread = sb("spread", 240)
        SELW = sb("select_wide", 240)
        SG = sb("select_group", P)
        XS = sb("select_tokens", P)
        QG = sb("group_queries_T", 2 * P)
        S0 = sb("scores", 2 * P)
        S1 = sb("scores_left", 2 * P)
        top = sb("top_values", 32)
        top_i = sb("top_index", 32, U32)
        top_f = sb("top_index_f", 32)
        cand = sb("candidates", 256)
        cand2 = sb("candidates_left", 256)
        best = sb("best", SEL)
        pick = sb("pick", SEL, U32)
        pick_a = sb("pick_a", 2 * SEL, U32)
        pick_f = sb("pick_f", 2 * SEL)
        OH = sb("one_hot", 2 * 256)
        id_f = sb("id_f", 3 * SEL)
        IDU = sb("ids_u", SEL, U32)
        IDV = sb("ids_v", SEL, U32)
        nb0 = sb("minus_best", 1)
        GE = sb("gate_exp", SEL)
        GS = sb("gate_sum", 2)
        GA = sb("gates", SEL)
        DOT = sb("dots", SEL)
        GL = sb("gelu", SEL)
        AV = sb("activations", SEL)
        SSQ = sb("sum_squares", 11)
        RS = sb("rstd", 11)
        hs = sb("head_sums", 40)
        MS = sb("mean_squares", 11)
        RT = sb("roots", 11)
        red = sb("reductions", 16)
        m8 = sb("max8", 8)

        s_x = sem("s_x")
        s_small = sem("s_small")
        s_win = [sem(f"s_win{c}") for c in range(KC)]
        s_awo = sem("s_awo")
        s_pq = [[sem(f"s_pq{l}{q}") for q in range(4)] for l in range(2)]
        s_grow = sem("s_grow")
        s_bwq = sem("s_bwq")
        s_kvw = sem("s_kvw")
        s_bwo = sem("s_bwo")
        s_const = sem("s_const")
        s_constp = sem("s_constp")
        s_tr = sem("s_tr")
        s_setup = sem("s_setup")
        s_ssq = sem("s_ssq")
        s_ms = sem("s_ms")
        s_root = sem("s_root")
        s_hms = sem("s_hms")
        s_hroot = sem("s_hroot")
        s_rstd = sem("s_rstd")
        s_xh = sem("s_xh")
        s_xhT = sem("s_xhT")
        s_xT = sem("s_xT")
        s_proj = sem("s_proj")
        s_pj = sem("s_pj")
        s_pjv = sem("s_pjv")
        s_roped = sem("s_roped")
        s_qkT = sem("s_qkT")
        s_qk = sem("s_qk")
        s_idx = sem("s_idx")
        s_relu = sem("s_relu")
        s_score = sem("s_score")
        s_causal = sem("s_causal")
        s_sel = sem("s_sel")
        s_bias = sem("s_bias")
        s_logit = sem("s_logit")
        s_zread = sem("s_zread")
        s_e1 = sem("s_e1")
        s_e2 = sem("s_e2")
        s_e3 = sem("s_e3")
        s_prob = sem("s_prob")
        s_PTp = sem("s_PTp")
        s_PT = sem("s_PT")
        s_pv = sem("s_pv")
        s_oT = sem("s_oT")
        s_wo = sem("s_wo")
        s_h = sem("s_h")
        s_rq = sem("s_rq")
        s_rqa = sem("s_rqa")
        s_rqd = sem("s_rqd")
        s_kvp = sem("s_kvp")
        s_kvs = sem("s_kvs")
        s_bq = sem("s_bq")
        s_bqs = sem("s_bqs")
        s_ab = sem("s_ab")
        s_mid1 = sem("s_mid1")
        s_mid2 = sem("s_mid2")
        s_sp = sem("s_sp")
        s_spm = sem("s_spm")
        s_lm = sem("s_lm")
        s_ld = [sem(f"s_ld{k}") for k in range(16)]
        s_QG = sem("s_QG")
        s_XS = sem("s_XS")
        s_xr = sem("s_xr")
        s_xru = sem("s_xru")
        s_s = sem("s_s")
        s_S = sem("s_S")
        s_best = sem("s_best")
        s_gexp = sem("s_gexp")
        s_IDU = sem("s_IDU")
        s_IDV = sem("s_IDV")
        s_dots = sem("s_dots")
        s_gelu = sem("s_gelu")
        s_act = sem("s_act")
        s_DG = sem("s_DG")
        s_vused = sem("s_vused")
        s_fin = sem("s_fin")
        s_out = sem("s_out")
        s_dve = sem("s_dve")
        s_actc = sem("s_actc")
        s_carry = sem("s_carry")

        NORM = {"a": [0, 1, 2], "f0": [3, 4, 5], "b": [6, 7, 8], "f1": [None, 9, 10]}
        XTC = {0: 2, 1: 4, 2: 6, 3: 8, 4: 10, 5: 12, 6: 14, 7: 18, 8: 22, 9: 24, 10: 26}
        GAIN = {"a": 0, "kv": 1, "b": 2, "f0": 3, "f1": 4}

        def group_no(layer, i, j):
            return (0 if i == 0 else 1 + 8 * (i - 1) + j) if layer == 0 else 17 + 8 * (i - 1) + j

        def schedule(up, vp, clear, fin, loop):
            def layer(l, first):
                prev = None
                for i in range(first, TILES):
                    up(l, i, 0)
                    if prev is not None:
                        vp(l, *prev)
                        fin(l, prev[0])
                    clear(l, i)
                    if i == 0:
                        prev = (0, 0)
                        continue
                    loop(l, i)
                    prev = (i, 7)
                vp(l, *prev)
                fin(l, prev[0])
            return layer

        block = ctx.enter_context(nc.Block())

        @block.sync
        def _(sp):
            sp.dma_start(hx[:META, 0, :], meta).then_inc(s_x, 16)
            for i in (1, 2):
                sp.dma_start(hx[:, i, :], x[0, (i - 1) * P:i * P, :]).then_inc(s_x, 16)
            for n, g in enumerate((a_norm[0], kv_norm, b_norm[0], ffn_norm[0], ffn_norm[1])):
                sp.dma_start(g_rows[8 * n:8 * n + 8, :], g.rearrange("(c p) -> c p", p=P)).then_inc(s_small, 16)
            sp.dma_start(sk_rows[:, :, :], peer_subkeys.rearrange("l c k d -> k (l c) d")).then_inc(s_small, 16)
            sp.dma_start(RO[:META, 0, :], rope[0:META, :]).then_inc(s_small, 16)
            sp.dma_start(RO[:, 1:3, :], rope[META:T, :].rearrange("(i p) c -> p i c", p=P)).then_inc(s_small, 16)
            sp.dma_start(qg[:, :], a_q_norm.broadcast_to([P, P])).then_inc(s_small, 16)
            sp.dma_start(kg[:, :], a_k_norm.broadcast_to([P, P])).then_inc(s_small, 16)
            w_rows = a_w_in[0].rearrange("(c p) n -> p c n", p=P)
            for c in range(KC):
                sp.dma_start(w_in[:, c, :], w_rows[:, c, :]).then_inc(s_win[c], 16)
            sp.dma_start(a_wo, a_w_o[0].rearrange("(h p) n -> p h n", p=P)).then_inc(s_awo, 16)
            pq_rows = [peer_w_q[l].rearrange("(c p) n -> p c n", p=P) for l in range(2)]

            def load_pq(l, q):
                sp.dma_start(pq[l][q], pq_rows[l][:, :, 512 * q:512 * q + 512]).then_inc(s_pq[l][q], 16)

            load_pq(0, 0)
            sp.dma_start(grow[:, :], ffn_norm[0:1].broadcast_to([P, D])).then_inc(s_grow, 16)
            sp.wait_ge(s_proj, 3)
            for q in (1, 2, 3):
                load_pq(0, q)
            sp.wait_ge(s_rq, 16)
            sp.dma_start(kv_ws, kv_w.rearrange("(c p) n -> p c n", p=P)).then_inc(s_kvw, 16)
            sp.dma_start(b_wq, b_w_q[0].rearrange("(c p) n -> p c n", p=P)).then_inc(s_bwq, 16)
            sp.wait_ge(s_fin, 3)
            sp.dma_start(b_wo, b_w_o[0].rearrange("(h p) n -> p h n", p=P)).then_inc(s_bwo, 16)
            for q in (0, 1):
                load_pq(1, q)
            sp.dma_start(grow[:, :], ffn_norm[1:2].broadcast_to([P, D])).then_inc(s_grow, 16)
            sp.wait_ge(s_bq, 8)
            for q in (2, 3):
                load_pq(1, q)
            for i in (1, 2):
                sp.wait_ge(s_fin, 3 + i)
                sp.dma_start(out[0, (i - 1) * P:i * P, :], hx[:, i, :]).then_inc(s_out, 16)
            sp.wait_ge(s_out, 32)

        @block.gpsimd
        def _(pool):
            pool.memset(ident[:, :], 0.0)
            pool.memset(spread[:, :], 0.0)
            pool.memset(zeros[:, :], 0.0)
            pool.memset(ones[:, :], 1.0)
            pool.memset(qt_t[:, :], 0.0)
            pool.memset(BIAS[:, :], 0.0)
            pool.iota(iota16[:, :], pattern=[[1, SEL]], base=0, channel_multiplier=0,
                      allow_small_or_imprecise_dtypes=True).then_inc(s_constp, 1)
            pool.wait_ge(s_constp, 1)
            pool.affine_select(out=ident[:, :], in_=ident[:, :], compare_op=ALU.not_equal, fill=1.0, base=0,
                               pattern=[[-1, P]], channel_multiplier=1).then_inc(s_constp, 1)
            pool.wait_ge(s_constp, 2)
            pool.tensor_copy(XS[:GT, :].rearrange("p (h t) -> p h t", t=GT),
                             ident[:GT, :GT].unsqueeze(1).broadcast_to([GT, HEADS, GT]))
            pool.affine_select(out=spread[:GT, :], in_=spread[:GT, :], compare_op=ALU.not_equal, fill=1.0,
                               base=112, pattern=[[-1, 240]], channel_multiplier=1)
            pool.affine_select(out=BIAS[:META, :META], in_=BIAS[:META, :META], compare_op=ALU.is_ge, fill=NEG,
                               base=0, pattern=[[-1, META]], channel_multiplier=1).then_inc(s_const, 1)

            def causal(ap, i, count, op, fill, s):
                keys = KEYS[i]
                pattern = [[-1, keys]] if count == 1 else [[0, count], [-1, keys]]
                pool.affine_select(out=ap, in_=ap, compare_op=op, fill=fill, base=OFF[i], pattern=pattern,
                                   channel_multiplier=1).then_inc(s, 1)

            for i in (1, 2):
                pool.wait_ge(s_score, i)
                causal(SC[:, :KEYS[i]], i, 1, ALU.is_ge, MASKED, s_causal)
                pool.wait_ge(s_sel, i)
                causal(BIAS[:, :KEYS[i]], i, 1, ALU.is_ge, NEG, s_bias)

            def gather(table, ids, k):
                pool.indirect_dma_start(
                    out=ring[:, k, :], out_offset=None, in_=table,
                    in_offset=bass.IndirectOffsetOnAxis(ap=ids[:, k:k + 1], axis=0)).then_inc(s_ld[k], 16)

            def up(l, i, j):
                n = group_no(l, i, j)
                pool.wait_ge(s_IDU, n + 1)
                pool.sem_inc(s_carry, 1)
                if l == 0 and i == 0:
                    pool.wait_ge(s_rq, 16)
                elif l == 1 and i == 1 and isinstance(j, int):
                    pool.wait_ge(s_rq, 32)
                for k in range(16):
                    if k % 4 == 0 and not (l == 0 and i == 0):
                        pool.wait_ge(s_vused, 16 * (n - 1) + k + 4)
                        pool.sem_inc(s_carry, 1)
                    gather(u_rows, IDU, k)

            def vp(l, i, j):
                n = group_no(l, i, j)
                pool.wait_ge(s_IDV, n + 1)
                pool.sem_inc(s_carry, 1)
                for k in range(16):
                    if k % 4 == 0:
                        pool.wait_ge(s_dots, 16 * n + k + 4)
                        pool.sem_inc(s_carry, 1)
                    gather(v_rows, IDV, k)

            def tile(l, i):
                with pool.Fori(1, 8) as j:
                    vp(l, i, j - 1)
                    up(l, i, j)

            def layer(l, first):
                prev = None
                for i in range(first, TILES):
                    if prev is not None:
                        vp(l, *prev)
                    up(l, i, 0)
                    if i:
                        tile(l, i)
                    prev = (i, 7 if i else 0)
                vp(l, *prev)

            layer(0, 0)
            for i in (1, 2):
                for g in range(KV):
                    u = 2 * (i - 1) + g
                    pool.wait_ge(s_sp, u + 1)
                    causal(E4[:, :, :KEYS[i]], i, GROUP, ALU.is_gt, 0.0, s_spm)
                    pool.wait_ge(s_ab, u + 1)
                    causal(L[:, :, :KEYS[i]], i, GROUP, ALU.is_gt, NEG, s_lm)
            layer(1, 1)

        @block.scalar
        def _(act):
            c = Chain(act, s_actc)
            A = act.activation
            act.wait_ge(s_x, 48)
            act.wait_ge(s_const, 1)

            def norm(kind, i):
                k, n = NORM[kind][i], NT[i]
                if k:
                    act.wait_ge(s_xhT, 2 * k)
                A(XR[:n, :], hx[:n, i, :], ACT.Square, accum_out=SSQ[:n, k:k + 1]).then_inc(s_ssq, 1)
                act.wait_ge(s_ms, k + 1)
                A(RT[:n, k:k + 1], MS[:n, k:k + 1], ACT.Sqrt).then_inc(s_root, 1)
                act.wait_ge(s_rstd, k + 1)
                A(XR[:n, :], hx[:n, i, :], ACT.Copy, scale=RS[:n, k:k + 1]).then_inc(s_xh, 1)

            def attend(t, i, b):
                n, keys = NT[i], KEYS[i]
                for g in range(KV):
                    u = 2 * t + g
                    if not b:
                        act.wait_ge(s_e1, u + 1)
                        A(L[:n, :, :keys], L[:n, :, :keys], ACT.Exp).then_inc(s_e2, 1)
                    else:
                        w = u - 6
                        act.wait_ge(s_e1, u + 1)
                        c.do(A(E4[:n, :, :keys], E4[:n, :, :keys], ACT.Exp, scale=-1.0))
                        A(E4[:n, :, :keys], E4[:n, :, :keys], ACT.Ln, bias=1.0).then_inc(s_e2, 1)
                        act.wait_ge(s_lm, w + 1)
                        A(L[:n, :, :keys], L[:n, :, :keys], ACT.Exp).then_inc(s_prob, 1)
                    act.wait_ge(s_pv, u + 1)
                    if g == 0 and t:
                        act.wait_ge(s_wo, t)
                    A(oT[:, GROUP * g:GROUP * (g + 1), :n],
                      bank[:, 7, :GROUP * n].rearrange("p (h n) -> p h n", n=n), ACT.Copy).then_inc(s_oT, 1)

            for i in range(TILES):
                n = NT[i]
                norm("a", i)
                act.wait_ge(s_proj, i + 1)
                if i:
                    act.wait_ge(s_qkT, i)
                A(PJ[:n, 0:8, :], bank[:n, 0:2, :].rearrange("p b (h d) -> p (b h) d", d=P), ACT.Copy).then_inc(s_pj, 1)
                act.wait_ge(s_hms, i + 1)
                A(hs[:n, 20:30], hs[:n, 0:10], ACT.Sqrt).then_inc(s_hroot, 1)
                if i:
                    act.wait_ge(s_idx, i)
                    A(R4[:n, :, :KEYS[i]], bank[:n, 0:4, :KEYS[i]], ACT.Relu, scale=IDX_SCALE).then_inc(s_relu, 1)
                attend(i, i, False)
            for i in range(TILES):
                act.wait_ge(s_h, i + 1)
                norm("f0", i)

            def router(l):
                ntok, o = (T, 0) if l == 0 else (2 * P, 1)
                for m in range(1, 16, 2):
                    act.wait_ge(s_rq, 16 * l + m + 1)
                    A(QTw[:, m % 2, o:o + ntok // GT, m // 2, :],
                      bank[:, m % 4, :ntok].rearrange("p (g t) -> p g t", t=GT), ACT.Copy).then_inc(s_rqa, 1)
                act.wait_ge(s_rqa, 8 * l + 8)
                act.wait_ge(s_rqd, 8 * l + 8)

            router(0)

            def up(l, i, j):
                n = group_no(l, i, j)
                r = NORM["f0" if l == 0 else "f1"][i]
                nt = NT[i]
                g = 0 if i == 0 else 1 + 8 * (i - 1) + j
                if not (isinstance(n, int) and n == 0):
                    act.wait_ge(s_s, n)
                    act.sem_inc(s_carry, 1)
                A(QG[:, :].rearrange("p (c m) -> p c m", c=2), QT[:, :, bass.ds(g, 1), :].rearrange("p c o m -> p c (o m)"),
                  ACT.Copy).then_inc(s_QG, 1)
                if not (isinstance(n, int) and n == 0):
                    act.wait_ge(s_xr, n)
                    act.sem_inc(s_carry, 1)
                A(XS[:nt, :].rearrange("p (h t) -> p h t", t=GT),
                  ident[:nt, bass.ds(16 * j, 16)].unsqueeze(1).broadcast_to([nt, HEADS, GT]),
                  ACT.Copy, scale=RS[:nt, r:r + 1]).then_inc(s_XS, 1)
                if not (isinstance(n, int) and n == 0):
                    act.wait_ge(s_DG, 16 * n)
                    act.sem_inc(s_carry, 1)
                c.do(A(SG[:, :], SELW[:, bass.ds(112 - 16 * j, P)], ACT.Copy))
                if not (isinstance(n, int) and n == 0):
                    act.wait_ge(s_IDU, n)
                act.wait_ge(s_s, n + 1)
                A(S0[:, :], bank[:, 2, 0:2 * P], ACT.Copy).then_inc(s_S, 1)
                act.wait_ge(s_best, n + 1)
                A(GE[:, :], best[:, :], ACT.Exp, bias=nb0[:, :], accum_out=GS[:, 0:1]).then_inc(s_gexp, 1)
                act.wait_ge(s_dots, 16 * n + 16)
                A(GL[:, :], DOT[:, :], ACT.Gelu).then_inc(s_gelu, 1)
                act.wait_ge(s_act, n + 1)
                if not (isinstance(n, int) and n == 0):
                    act.wait_ge(s_vused, 16 * n)
                for k in range(16):
                    A(DG[:, k, :], SG[:, :], ACT.Copy, scale=AV[:, k:k + 1]).then_inc(s_DG, 1)

            def layer(l, first):
                for i in range(first, TILES):
                    up(l, i, 0)
                    if i:
                        c_n = c.n
                        with act.Fori(1, 8) as j:
                            c.off = j - 1
                            up(l, i, j)
                        c.n, c.off = c_n + 7, 0

            layer(0, 0)
            act.wait_ge(s_fin, 3)
            for i in range(TILES):
                norm("b", i)
            for i in range(TILES):
                act.wait_ge(s_kvp, 2 + i + 1)
                A(V[:NT[i], i, :], bank[:NT[i], 2 + i % 2, 0:256], ACT.Copy).then_inc(s_kvs, 1)
            for i in (1, 2):
                attend(2 + i, i, True)
            for i in (1, 2):
                act.wait_ge(s_h, 3 + i)
                norm("f1", i)
            router(1)
            layer(1, 1)

        @block.vector
        def _(dve):
            c = Chain(dve, s_dve)
            tt, ts, stt = dve.tensor_tensor, dve.tensor_scalar, dve.scalar_tensor_tensor

            dve.wait_ge(s_tr, 1)
            dve.tensor_copy(gcol[:, :], bank[:, 0, 0:40])
            dve.tensor_copy(skT[:, :, :], bank[:, 1, :].rearrange("p (m k) -> p m k", k=P))
            dve.tensor_copy(SELW[:, :], bank[:, 2, 0:240]).then_inc(s_setup, 1)
            dve.wait_ge(s_setup, 1)
            dve.wait_ge(s_small, 160)

            def inverse_root(dst, ms, root, tmp):
                c.do(dve.reciprocal(dst, root))
                c.do(tt(tmp, ms, dst, ALU.mult))
                c.do(tt(tmp, tmp, dst, ALU.mult))
                c.do(ts(tmp, tmp, -0.5, 1.5, ALU.mult, ALU.add))
                return tt(dst, dst, tmp, ALU.mult)

            def norm(kind, i):
                k, n, o = NORM[kind][i], NT[i], OFF[i]
                dve.wait_ge(s_ssq, k + 1)
                ts(MS[:n, k:k + 1], SSQ[:n, k:k + 1], 1.0 / D, EPS, ALU.mult, ALU.add).then_inc(s_ms, 1)
                dve.wait_ge(s_root, k + 1)
                inverse_root(RS[:n, k:k + 1], MS[:n, k:k + 1], RT[:n, k:k + 1], hs[:n, 0:1]).then_inc(s_rstd, 1)
                outs = {"b": [("kv", xT2)] + ([("b", xT)] if i else [])}.get(kind, [(kind, xT)])
                for half in range(2):
                    dve.wait_ge(s_xhT, 2 * k + half + 1)
                    src = bank[:, 4 + half, :4 * n].rearrange("p (c n) -> p c n", n=n)
                    for gain, dst in outs:
                        a = GAIN[gain] * 8 + 4 * half
                        tt(dst[:, 4 * half:4 * half + 4, o:o + n], src,
                           gcol[:, a:a + 4].unsqueeze(2).broadcast_to([P, 4, n]), ALU.mult).then_inc(s_xT, 1)

            def rotate(view, i, half, at, heads):
                n = NT[i]
                cos = RO[:n, i, at:at + half].unsqueeze(1).broadcast_to([n, heads, half])
                sin = RO[:n, i, at + half:at + 2 * half].unsqueeze(1).broadcast_to([n, heads, half])
                a, b = view[:, :, 0:half], view[:, :, half:2 * half]
                w = heads * half
                t = [TMP[:n, m * w:(m + 1) * w].rearrange("p (h d) -> p h d", d=half) for m in range(4)]
                tt(t[0], a, cos, ALU.mult)
                tt(t[1], b, sin, ALU.mult)
                tt(t[2], b, cos, ALU.mult)
                c.do(tt(t[3], a, sin, ALU.mult))
                tt(a, t[0], t[1], ALU.subtract)
                return tt(b, t[2], t[3], ALU.add)

            def project_a(i):
                n = NT[i]
                dve.wait_ge(s_proj, i + 1)
                dve.tensor_copy(PJ[:n, 8:10, :], bank[:n, 2, 0:256].rearrange("p (b d) -> p b d", d=P))
                dve.tensor_copy(V[:n, i, :], bank[:n, 2, 256:512])
                dve.tensor_copy(PJ[:n, 12:14, :], bank[:n, 3, 0:256].rearrange("p (b d) -> p b d", d=P))
                dve.tensor_copy(PJ[:n, 14, 0:64], bank[:n, 3, 256:320])
                c.do(dve.tensor_copy(WI[:n, :], bank[:n, 3, 320:324]))
                dve.wait_ge(s_pj, i + 1)
                qk = PJ[:n, 0:10, :]
                sq = TMP[:n, :].rearrange("p (h d) -> p h d", d=P)
                c.do(tt(sq, qk, qk, ALU.mult))
                c.do(dve.reduce_sum(hs[:n, 0:10], sq, AX.X))
                ts(hs[:n, 0:10], hs[:n, 0:10], 1.0 / P, EPS, ALU.mult, ALU.add).then_inc(s_hms, 1)
                dve.wait_ge(s_hroot, i + 1)
                c.do(inverse_root(hs[:n, 10:20], hs[:n, 0:10], hs[:n, 20:30], hs[:n, 30:40]))
                c.do(tt(qk, qk, hs[:n, 10:20].unsqueeze(2).broadcast_to([n, 10, P]), ALU.mult))
                tt(PJ[:n, 0:8, :], PJ[:n, 0:8, :], qg[:n, :].unsqueeze(1).broadcast_to([n, 8, P]), ALU.mult)
                c.do(tt(PJ[:n, 8:10, :], PJ[:n, 8:10, :], kg[:n, :].unsqueeze(1).broadcast_to([n, 2, P]), ALU.mult))
                c.do(rotate(qk, i, 16, 0, 10))
                qi = qt_t[:n, 12 * P:12 * P + 320].rearrange("p (h d) -> p h d", d=64)
                c.do(rotate(qi, i, 8, 32, 5))
                dve.tensor_copy(PJ[:n, 14, 64:128], PJ[:n, 14, 0:64]).then_inc(s_roped, 1)
                dve.wait_ge(s_qkT, i + 1)
                dve.tensor_copy(qT[:, :, :n], bank[:, 4:6, :4 * n].rearrange("p b (h n) -> p (b h) n", n=n)
                                if n == P else bank[:, 4, :8 * n].rearrange("p (h n) -> p h n", n=n))
                src = bank[:, 6, :5 * n].rearrange("p (h n) -> p h n", n=n) if n < P else None
                if n == P:
                    dve.tensor_copy(kT[:, :, OFF[i]:OFF[i] + n], bank[:, 6, 0:256].rearrange("p (h n) -> p h n", n=n))
                    dve.tensor_copy(qiT[:, :, :n], bank[:, 6, 256:512].rearrange("p (h n) -> p h n", n=n))
                    dve.tensor_copy(kiT[:, OFF[i]:OFF[i] + n], bank[:, 7, 0:n]).then_inc(s_qk, 1)
                else:
                    dve.tensor_copy(kT[:, :, :n], src[:, 0:2, :])
                    dve.tensor_copy(kiT[:, :n], src[:, 4, :]).then_inc(s_qk, 1)

            def select(i):
                n, keys = NT[i], KEYS[i]
                dve.wait_ge(s_relu, i)
                c.do(ts(SC[:n, :keys], R4[:n, 0, :keys], WI[:n, 0:1], None, ALU.mult))
                for h in range(1, IDX_HEADS):
                    ins = stt(SC[:n, :keys], R4[:n, h, :keys], WI[:n, h:h + 1], SC[:n, :keys], ALU.mult, ALU.add)
                    if h < IDX_HEADS - 1:
                        c.do(ins)
                    else:
                        ins.then_inc(s_score, 1)
                dve.wait_ge(s_causal, i)
                src = SC
                for r in range(TOPK // 8):
                    c.do(dve.max(m8[:n, :], src[:n, :keys]))
                    dst = WK if r % 2 == 0 else SC
                    c.do(dve.match_replace(dst[:n, :keys], m8[:n, :], src[:n, :keys], TAKEN))
                    src = dst
                if i == 1:
                    dve.wait_ge(s_e2, 2)
                ts(BIAS[:n, :keys], src[:n, :keys], TAKEN_BELOW, NEG, ALU.is_gt, ALU.mult).then_inc(s_sel, 1)

            def heads_out(t, i, u):
                n = NT[i]
                dve.wait_ge(s_PTp, u + 1)
                for j in range(i + 1):
                    kn = NT[j]
                    ins = dve.tensor_copy(PT[:kn, j, :GROUP * n], bank[:kn, 4 + j, :GROUP * n])
                ins.then_inc(s_PT, 1)

            def residual(t, i):
                n = NT[i]
                dve.wait_ge(s_wo, t + 1)
                tt(hx[:n, i, :], hx[:n, i, :], bank[:n, 4:6, :].rearrange("p b n -> p (b n)"), ALU.add).then_inc(s_h, 1)

            def attend_a(t, i):
                n, keys = NT[i], KEYS[i]
                if i:
                    dve.wait_ge(s_bias, i)
                for g in range(KV):
                    u = 2 * t + g
                    dve.wait_ge(s_logit, u + 1)
                    if u:
                        dve.wait_ge(s_PTp, u)
                    z = L[:n, :, :keys]
                    stt(z, bank[:n, 0:4, :keys], SCALE, BIAS[:n, :keys].unsqueeze(1).broadcast_to([n, GROUP, keys]),
                        ALU.mult, ALU.add).then_inc(s_zread, 1)
                    dve.wait_ge(s_zread, u + 1)
                    c.do(dve.reduce_max(red[:n, 0:4], z, AX.X))
                    tt(z, z, red[:n, 0:4].unsqueeze(2).broadcast_to([n, GROUP, keys]), ALU.subtract).then_inc(s_e1, 1)
                    dve.wait_ge(s_e2, u + 1)
                    c.do(dve.reduce_sum(red[:n, 4:8], z, AX.X))
                    c.do(dve.reciprocal(red[:n, 8:12], red[:n, 4:8]))
                    tt(z, z, red[:n, 8:12].unsqueeze(2).broadcast_to([n, GROUP, keys]), ALU.mult).then_inc(s_prob, 1)
                    heads_out(t, i, u)
                residual(t, i)

            for i in range(TILES):
                norm("a", i)
                project_a(i)
                if i:
                    select(i)
                attend_a(i, i)
            for i in range(TILES):
                norm("f0", i)

            def router(l):
                ntok, o = (T, 0) if l == 0 else (2 * P, 1)
                for m in range(0, 16, 2):
                    dve.wait_ge(s_rq, 16 * l + m + 1)
                    dve.tensor_copy(QTw[:, m % 2, o:o + ntok // GT, m // 2, :],
                                    bank[:, m % 4, :ntok].rearrange("p (g t) -> p g t", t=GT)).then_inc(s_rqd, 1)

            router(0)
            dve.wait_ge(s_grow, 16)

            def up(l, i, j):
                n = group_no(l, i, j)
                later = not (isinstance(n, int) and n == 0)

                def carry():
                    dve.sem_inc(s_carry, 1)

                dve.wait_ge(s_xr, n + 1)
                tt(XR[:, :], bank[:, 0:2, :].rearrange("p b n -> p (b n)"), grow[:, :], ALU.mult).then_inc(s_xru, 1)
                dve.wait_ge(s_S, n + 1)
                carry()
                for h in range(2):
                    s = slice(P * h, P * h + P)
                    ins = dve.max(top[:, 16 * h:16 * h + 8], S0[:, s])
                c.do(ins)
                carry()
                for h in range(2):
                    s, t = slice(P * h, P * h + P), slice(16 * h, 16 * h + 8)
                    dve.max_index(top_i[:, t], top[:, t], S0[:, s])
                    ins = dve.match_replace(S1[:, s], top[:, t], S0[:, s], TAKEN)
                c.do(ins)
                carry()
                for h in range(2):
                    s = slice(P * h, P * h + P)
                    ins = dve.max(top[:, 16 * h + 8:16 * h + 16], S1[:, s])
                c.do(ins)
                carry()
                for h in range(2):
                    s, t = slice(P * h, P * h + P), slice(16 * h + 8, 16 * h + 16)
                    dve.max_index(top_i[:, t], top[:, t], S1[:, s])
                a = top[:, 0:16].unsqueeze(2).broadcast_to([P, 16, 16])
                b = top[:, 16:32].unsqueeze(1).broadcast_to([P, 16, 16])
                c.do(tt(cand[:, :].rearrange("p (a b) -> p a b", b=16), a, b, ALU.add))
                carry()
                c.do(dve.max(best[:, 0:8], cand[:, :]))
                carry()
                dve.max_index(pick[:, 0:8], best[:, 0:8], cand[:, :])
                c.do(dve.match_replace(cand2[:, :], best[:, 0:8], cand[:, :], TAKEN))
                carry()
                c.do(dve.max(best[:, 8:16], cand2[:, :]))
                carry()
                dve.max_index(pick[:, 8:16], best[:, 8:16], cand2[:, :])
                ts(nb0[:, :], best[:, 0:1], -1.0, None, ALU.mult).then_inc(s_best, 1)
                dve.wait_ge(s_best, n + 1)
                ts(pick_a[:, 0:16], pick[:, :], 4, None, ALU.logical_shift_right)
                ts(pick_a[:, 16:32], pick[:, :], 15, None, ALU.bitwise_and)
                c.do(dve.tensor_copy(top_f[:, :], top_i[:, :]))
                c.do(dve.tensor_copy(pick_f[:, :], pick_a[:, :]))
                oh = OH[:, :].rearrange("p (k a) -> p k a", a=16)
                c.do(tt(oh, pick_f[:, :].unsqueeze(2).broadcast_to([P, 32, 16]),
                        iota16[:, :].unsqueeze(1).broadcast_to([P, 32, 16]), ALU.is_equal))
                for h in range(2):
                    ins = tt(oh[:, 16 * h:16 * h + 16, :], oh[:, 16 * h:16 * h + 16, :],
                             top_f[:, 16 * h:16 * h + 16].unsqueeze(1).broadcast_to([P, 16, 16]), ALU.mult)
                c.do(ins)
                c.do(dve.reduce_sum(id_f[:, 0:32], oh, AX.X))
                c.do(stt(id_f[:, 32:48], id_f[:, 0:16], float(NKEYS), id_f[:, 16:32], ALU.mult, ALU.add))
                ts(IDU[:, :], id_f[:, 32:48], float(EXPERTS * l), None, ALU.add).then_inc(s_IDU, 1)
                dve.wait_ge(s_gexp, n + 1)
                c.do(dve.reciprocal(GS[:, 1:2], GS[:, 0:1]))
                c.do(ts(GA[:, :], GE[:, :], GS[:, 1:2], None, ALU.mult))
                for k in range(16):
                    dve.wait_ge(s_ld[k], 16 * (2 * n + 1))
                    stt(ring[:, k, :], ring[:, k, :], 1.0, XR[:, :], ALU.mult, ALU.mult,
                        accum_out=DOT[:, k:k + 1]).then_inc(s_dots, 1)
                if later:
                    dve.wait_ge(s_vused, 16 * n)
                dve.wait_ge(s_IDU, n + 1)
                dve.tensor_copy(IDV[:, :], IDU[:, :]).then_inc(s_IDV, 1)
                dve.wait_ge(s_IDV, n + 1)
                dve.wait_ge(s_gelu, n + 1)
                if later:
                    dve.wait_ge(s_DG, 16 * n)
                tt(AV[:, :], GL[:, :], GA[:, :], ALU.mult).then_inc(s_act, 1)
                dve.wait_ge(s_act, n + 1)

            def fin(l, i):
                n, last = NT[i], group_no(l, i, 7)
                dve.wait_ge(s_vused, 16 * (last + 1))
                tt(hx[:n, i, :], hx[:n, i, :], bank[:n, 6:8, :].rearrange("p b n -> p (b n)"), ALU.add).then_inc(s_fin, 1)

            def layer(l, first):
                prev = None
                for i in range(first, TILES):
                    up(l, i, 0)
                    if prev is not None:
                        fin(l, prev)
                    if i:
                        start = c.n
                        per = UP_STEPS
                        with dve.Fori(1, 8) as j:
                            c.off = (j - 1) * per
                            up(l, i, j)
                        assert c.n - start == per, c.n - start
                        c.n, c.off = start + 7 * per, 0
                    prev = i
                fin(l, prev)

            layer(0, 0)
            dve.wait_ge(s_fin, 3)
            for i in range(TILES):
                norm("b", i)
            for g in range(KV):
                dve.wait_ge(s_kvp, g + 1)
                dve.tensor_copy(kT[:, g, :], bank[:, g, :T]).then_inc(s_mid1, 1)
            for h in range(HEADS):
                dve.wait_ge(s_bq, h + 1)
                dve.tensor_copy(qTB[:, h, :], bank[:, h % 4, 0:2 * P]).then_inc(s_bqs, 1)

            def attend_b(t, i):
                n, keys = NT[i], KEYS[i]
                for g in range(KV):
                    u = 2 * t + g
                    w = u - 6
                    z, e, cs = L[:n, :, :keys], E4[:n, :, :keys], C4[:n, :, :keys]
                    dve.wait_ge(s_logit, u + 1)
                    dve.wait_ge(s_PTp, u)
                    ts(z, bank[:n, 0:4, :keys], SCALE, None, ALU.mult).then_inc(s_zread, 1)
                    dve.wait_ge(s_zread, u + 1)
                    stt(e, z, -1.0, z, ALU.mult, ALU.max).then_inc(s_e1, 1)
                    dve.wait_ge(s_e2, u + 1)
                    stt(e, z, 0.0, e, ALU.max, ALU.add).then_inc(s_sp, 1)
                    dve.wait_ge(s_spm, w + 1)
                    for h in range(GROUP):
                        ins = dve.tensor_tensor_scan(C4[:n, h, keys - 1::-1] if keys == T else C4[:n, h, 0:keys][:, ::-1],
                                                     ones[:n, :keys], E4[:n, h, 0:keys][:, ::-1], 0.0, ALU.mult, ALU.add)
                    c.do(ins)
                    tt(z, z, cs, ALU.subtract).then_inc(s_ab, 1)
                    heads_out(t, i, u)
                residual(t, i)

            for i in (1, 2):
                attend_b(2 + i, i)
            for i in (1, 2):
                norm("f1", i)
            router(1)
            dve.wait_ge(s_grow, 32)
            layer(1, 1)

        @block.tensor
        def _(pe):
            mm = pe.matmul

            def put(dst, src):
                return pe.transpose(dst, src, ident[:src.shape[0], :src.shape[0]])

            pe.wait_ge(s_const, 1)
            pe.wait_ge(s_small, 160)
            put(bank[:, 0, 0:40], g_rows[:40, :])
            for m in range(4):
                put(bank[:, 1, P * m:P * m + P], sk_rows[:, m, :])
            mm(bank[:, 2, 0:240], XS[:GT, :], spread[:GT, :],
               start=True, stop=True).then_inc(s_tr, 1)
            pe.wait_ge(s_setup, 1)

            def norm(kind, i):
                k, n = NORM[kind][i], NT[i]
                pe.wait_ge(s_xh, k + 1)
                for half in range(2):
                    if k:
                        pe.wait_ge(s_xT, XTC[k - 1])
                    for m in range(4):
                        cc = 4 * half + m
                        ins = put(bank[:, 4 + half, m * n:m * n + n], XR[:n, P * cc:P * cc + P])
                    ins.then_inc(s_xhT, 1)

            def attend(t, i, q_of):
                n, keys = NT[i], KEYS[i]
                for g in range(KV):
                    u = 2 * t + g
                    if u:
                        pe.wait_ge(s_zread, u)
                    for h in range(GROUP):
                        ins = mm(bank[:n, h, :keys], q_of(GROUP * g + h), kT[:, g, :keys], start=True, stop=True)
                    ins.then_inc(s_logit, 1)
                    pe.wait_ge(s_prob, u + 1)
                    if u:
                        pe.wait_ge(s_PT, u)
                    for j in range(i + 1):
                        for h in range(GROUP):
                            ins = put(bank[:, 4 + j, h * n:h * n + n], L[:n, h, OFF[j]:OFF[j] + P])
                    ins.then_inc(s_PTp, 1)
                    pe.wait_ge(s_PT, u + 1)
                    if u:
                        pe.wait_ge(s_oT, u)
                    for j in range(i + 1):
                        kn = NT[j]
                        ins = mm(bank[:, 7, :GROUP * n], V[:kn, j, P * g:P * g + P], PT[:kn, j, :GROUP * n],
                                 start=j == 0, stop=j == i)
                    ins.then_inc(s_pv, 1)
                pe.wait_ge(s_oT, 2 * t + 2)

            def project_out(t, i, w):
                n = NT[i]
                for m in range(2):
                    for h in range(HEADS):
                        ins = mm(bank[:n, 4 + m, :], oT[:, h, :n], w[:, h, 512 * m:512 * m + 512],
                                 start=h == 0, stop=h == HEADS - 1)
                ins.then_inc(s_wo, 1)

            for i in range(TILES):
                n = NT[i]
                if i:
                    pe.wait_ge(s_h, i)
                norm("a", i)
                pe.wait_ge(s_xT, XTC[i])
                if i:
                    pe.wait_ge(s_zread, 2 * i)
                for cc in range(KC):
                    if i == 0:
                        pe.wait_ge(s_win[cc], 16)
                    for m in range(4):
                        w = min(512, A_COLS - 512 * m)
                        ins = mm(bank[:n, m, :w], xT[:, cc, OFF[i]:OFF[i] + n], w_in[:, cc, 512 * m:512 * m + w],
                                 start=cc == 0, stop=cc == KC - 1)
                ins.then_inc(s_proj, 1)
                pe.wait_ge(s_roped, i + 1)
                for h in range(8):
                    a = h * n
                    put(bank[:, 4 + a // 512, a % 512:a % 512 + n], PJ[:n, h, :])
                for m, b in enumerate((8, 9, 12, 13, 14)):
                    a = m * n
                    ins = put(bank[:, 6 + a // 512, a % 512:a % 512 + n], PJ[:n, b, :])
                ins.then_inc(s_qkT, 1)
                pe.wait_ge(s_qk, i + 1)
                if i:
                    for h in range(IDX_HEADS):
                        r = slice(64 * (h % 2), 64 * (h % 2) + 64)
                        ins = mm(bank[:n, h, :KEYS[i]], qiT[r, h // 2, :n], kiT[r, :KEYS[i]], start=True, stop=True)
                    ins.then_inc(s_idx, 1)
                    pe.wait_ge(s_relu, i)
                attend(i, i, lambda h: qT[:, h, :n])
                if i == 0:
                    pe.wait_ge(s_awo, 16)
                project_out(i, i, a_wo)
            pe.wait_ge(s_h, 3)
            for i in range(TILES):
                norm("f0", i)

            def router(l):
                ntok = T if l == 0 else 2 * P
                for m in range(16):
                    if m % 4 == 0:
                        pe.wait_ge(s_pq[l][m // 4], 16)
                    if m >= 4:
                        pe.wait_ge(s_rqa if m % 2 else s_rqd, 8 * l + (m - 4) // 2 + 1)
                    for cc in range(KC):
                        ins = mm(bank[:, m % 4, :ntok], pq[l][m // 4][:, cc, P * (m % 4):P * (m % 4) + P],
                                 xT[:, cc, T - ntok:T], start=cc == 0, stop=cc == KC - 1)
                    ins.then_inc(s_rq, 1)

            pe.wait_ge(s_xT, XTC[5])
            router(0)

            def up(l, i, j):
                n = group_no(l, i, j)
                nt = NT[i]
                pe.wait_ge(s_XS, n + 1)
                if not (isinstance(n, int) and n == 0):
                    pe.wait_ge(s_xru, n)
                else:
                    pe.wait_ge(s_rqa, 8)
                    pe.wait_ge(s_rqd, 8)
                for m in range(2):
                    ins = mm(bank[:, m, :], XS[:nt, :], hx[:nt, i, 512 * m:512 * m + 512], start=True, stop=True)
                ins.then_inc(s_xr, 1)
                pe.wait_ge(s_QG, n + 1)
                if not (isinstance(n, int) and n == 0):
                    pe.wait_ge(s_S, n)
                for h in range(2):
                    ins = mm(bank[:, 2, P * h:P * h + P], QG[:, P * h:P * h + P], skT[:, 2 * l + h, :],
                             start=True, stop=True)
                ins.then_inc(s_s, 1)

            def clear(l, i):
                if l or i:
                    pe.wait_ge(s_fin, i if l == 0 else i + 2)
                for m in range(2):
                    mm(bank[:, 6 + m, :].rearrange("p (a b) -> p a b", b=P), zeros[:, :], zeros[:, :].unsqueeze(1).broadcast_to([P, 4, P]), start=True, stop=False,
                       skip_group_check=True)

            def vp(l, i, j):
                n = group_no(l, i, j)
                pe.wait_ge(s_DG, 16 * n + 16)
                for k in range(16):
                    pe.wait_ge(s_ld[k], 16 * (2 * n + 2))
                    for m in range(2):
                        ins = mm(bank[:, 6 + m, :], DG[:, k, :], ring[:, k, 512 * m:512 * m + 512],
                                 start=False, stop=False, skip_group_check=True)
                    ins.then_inc(s_vused, 1)

            def layer(l, first):
                prev = None
                for i in range(first, TILES):
                    up(l, i, 0)
                    if prev is not None:
                        vp(l, *prev)
                    clear(l, i)
                    if i:
                        with pe.Fori(1, 8) as j:
                            up(l, i, j)
                            vp(l, i, j - 1)
                    prev = (i, 7 if i else 0)
                vp(l, *prev)

            layer(0, 0)
            pe.wait_ge(s_fin, 3)
            for i in range(TILES):
                norm("b", i)
            pe.wait_ge(s_xT, XTC[8])
            pe.wait_ge(s_kvw, 16)
            for g in range(KV):
                for cc in range(KC):
                    ins = mm(bank[:, g, :T], kv_ws[:, cc, P * g:P * g + P], xT2[:, cc, :],
                             start=cc == 0, stop=cc == KC - 1)
                ins.then_inc(s_kvp, 1)
            for i in range(TILES):
                n = NT[i]
                if i == 2:
                    pe.wait_ge(s_kvs, 1)
                for cc in range(KC):
                    ins = mm(bank[:n, 2 + i % 2, 0:256], xT2[:, cc, OFF[i]:OFF[i] + n], kv_ws[:, cc, 256:512],
                             start=cc == 0, stop=cc == KC - 1)
                ins.then_inc(s_kvp, 1)
            pe.wait_ge(s_bwq, 16)
            pe.wait_ge(s_mid1, 2)
            pe.wait_ge(s_kvs, 3)
            for h in range(HEADS):
                if h >= 4:
                    pe.wait_ge(s_bqs, h - 3)
                for cc in range(KC):
                    ins = mm(bank[:, h % 4, 0:2 * P], b_wq[:, cc, P * h:P * h + P], xT[:, cc, META:T],
                             start=cc == 0, stop=cc == KC - 1)
                ins.then_inc(s_bq, 1)
            pe.wait_ge(s_bqs, 8)
            for i in (1, 2):
                attend(2 + i, i, lambda h: qTB[:, h, P * (i - 1):P * i])
                if i == 1:
                    pe.wait_ge(s_bwo, 16)
                project_out(2 + i, i, b_wo)
                pe.wait_ge(s_h, 3 + i)
            for i in (1, 2):
                norm("f1", i)
            pe.wait_ge(s_xT, XTC[10])
            router(1)
            pe.wait_ge(s_rqa, 16)
            pe.wait_ge(s_rqd, 16)
            layer(1, 1)


UP_STEPS = 15

_INS = ["x", "meta_tokens", "a_norm", "a_w_in", "a_q_norm", "a_k_norm", "a_w_o", "kv_norm", "kv_w", "b_norm",
        "b_w_q", "b_w_o", "ffn_norm", "peer_w_q", "peer_subkeys", "peer_u", "peer_v"]


def _rope_table():
    import numpy as np
    pos = np.arange(T, dtype=np.float32)
    cols = []
    for r in (32, 16):
        inv = np.float32(500000.0) ** (-np.arange(r // 2, dtype=np.float32) * np.float32(2.0) / np.float32(r))
        ang = pos[:, None] * inv[None, :].astype(np.float32)
        cols += [np.cos(ang), np.sin(ang)]
    return np.ascontiguousarray(np.concatenate(cols, axis=1).astype(np.float32))


def kernel(**inputs):
    import numpy as _np
    import concourse.bacc as _bacc
    from concourse import mybir as _mybir
    from concourse.bass_utils import run_bass_kernel_spmd as _run

    nc = _bacc.Bacc("TRN2", target_bir_lowering=False, num_devices=1)
    arrays, args = {}, []
    for name in _INS + ["rope"]:
        a = _rope_table() if name == "rope" else _np.ascontiguousarray(inputs[name])
        arrays[f"in_{name}_dram"] = a
        args.append(nc.dram_tensor(f"in_{name}_dram", a.shape, _mybir.dt.from_np(a.dtype), kind="ExternalInput").ap())
    args.append(nc.dram_tensor("out_0_dram", (1, 2 * P, D), F32, kind="ExternalOutput").ap())
    build(nc, *args)
    r = _run(nc, [arrays], core_ids=[0])
    return r.results[0]["out_0_dram"]
```

```python
from contextlib import ExitStack

import concourse.bass as bass
from concourse import mybir

F32 = mybir.dt.float32
U32 = mybir.dt.uint32
ALU = mybir.AluOpType
ACT = mybir.ActivationFunctionType
AX = mybir.AxisListType

P = 128
D = 1024
KC = D // P
META = 16
TILES = 3
NT = [META, P, P]
OFF = [0, META, META + P]
T = META + 2 * P
KEYS = [META, META + P, T]
HEADS = 8
KV = 2
GROUP = HEADS // KV
IDX_HEADS = 4
TOPK = 64
A_COLS = 1860
EXPERTS = 16384
NKEYS = 128
SEL = 16
GT = 16
SCALE = 128.0 ** -0.5
IDX_SCALE = 1.0 / 16.0
EPS = 1e-6
NEG = -1.0e30
MASKED = -3.0e38
TAKEN = -3.4e38
TAKEN_BELOW = -3.2e38
WB = 6
XC = META + P
UP_STEPS = 15


class Chain:

    def __init__(self, eng, sem):
        self.eng, self.sem, self.n, self.off = eng, sem, 0, 0

    def do(self, ins):
        self.n += 1
        ins.then_inc(self.sem, 1)
        self.eng.wait_ge(self.sem, self.n + self.off)


def build(nc, x, meta, a_norm, a_w_in, a_q_norm, a_k_norm, a_w_o, kv_norm, kv_w, b_norm, b_w_q, b_w_o,
          ffn_norm, peer_w_q, peer_subkeys, peer_u, peer_v, rope, out):
    u_rows = peer_u.rearrange("l e d -> (l e) d")
    v_rows = peer_v.rearrange("l e d -> (l e) d")
    with ExitStack() as ctx:
        def sb(name, cols, dt=F32, rows=P):
            return ctx.enter_context(nc.sbuf_tensor(name, [rows, cols], dt))

        def sem(name):
            return ctx.enter_context(nc.semaphore(name))

        bank = ctx.enter_context(nc.psum_tensor("banks", [P, 8, 512], F32))

        arena = sb("arena", 16 * D)
        ring = arena[:, :].rearrange("p (k d) -> p k d", d=D)
        w_in = arena[:, 0:KC * A_COLS].rearrange("p (c n) -> p c n", n=A_COLS)
        wb_t = sb("weight_blocks", WB * D)
        wb = wb_t[:, :].rearrange("p (s c n) -> p s c n", s=WB, n=P)

        hx_t = sb("residual", TILES * D)
        hx = hx_t[:, :].rearrange("p (i d) -> p i d", d=D)
        x1_t = sb("x_norm_T", KC * XC)
        xT = x1_t[:, :].rearrange("p (c n) -> p c n", n=XC)
        x2_t = sb("kv_norm_T", KC * XC)
        xT2 = x2_t[:, :].rearrange("p (c n) -> p c n", n=XC)
        qt_t = sb("queries_T", 2 * 17 * P)
        QT = qt_t[:, :].rearrange("p (c g m) -> p c g m", c=2, m=P)
        QTw = qt_t[:, :].rearrange("p (c g h t) -> p c g h t", c=2, h=HEADS, t=GT)
        dg_t = sb("diagonals", 16 * P)
        DG = dg_t[:, :].rearrange("p (k m) -> p k m", m=P)
        PJt = [qt_t[:, 1920:3840], qt_t[:, 0:1920], dg_t[:, 0:1920]]
        PJ = [a.rearrange("p (b d) -> p b d", d=P) for a in PJt]
        l_t = sb("logits", GROUP * T)
        L = l_t[:, :].rearrange("p (h k) -> p h k", k=T)
        e_t = sb("softplus", GROUP * T)
        E4 = e_t[:, :].rearrange("p (h k) -> p h k", k=T)
        SC, WK = e_t[:, 0:T], e_t[:, T:2 * T]
        r_t = sb("index_scores", GROUP * T)
        R4 = r_t[:, :].rearrange("p (h k) -> p h k", k=T)
        C4 = R4
        q_t = [sb("q_T0", HEADS * META), sb("q_T1", HEADS * P), sb("q_T2", HEADS * P)]
        qT = [a[:, :].rearrange("p (h n) -> p h n", h=HEADS) for a in q_t]
        pt_t = sb("weights_T", 3 * 512)
        PT = pt_t[:, :].rearrange("p (j m) -> p j m", m=512)
        TMP = pt_t[:, 0:1280]
        o_t = [sb("heads_T0", HEADS * META), sb("heads_T", HEADS * P)]
        oT = [a[:, :].rearrange("p (h n) -> p h n", h=HEADS) for a in o_t]
        oT = [oT[0], oT[1], oT[1]]
        XR = sb("x_rows", D)
        XH = sb("x_norm", D)
        grow = [sb(f"ffn_gain_row{l}", D) for l in range(2)]
        V_t = sb("values", TILES * 256)
        V = V_t[:, :].rearrange("p (i d) -> p i d", d=256)
        kT_t = sb("keys_T", KV * T)
        kT = kT_t[:, :].rearrange("p (g k) -> p g k", k=T)
        kiT = sb("index_keys_T", T)
        qi_t = [None, sb("index_queries_T1", 2 * P), sb("index_queries_T2", 2 * P)]
        qiT = [None] + [a[:, :].rearrange("p (a n) -> p a n", n=P) for a in qi_t[1:]]
        WI_t = sb("index_weights", TILES * IDX_HEADS)
        WI = WI_t[:, :].rearrange("p (i h) -> p i h", i=TILES)
        BIAS = sb("bias", T)
        LATER = sb("later", T + 1)
        rope_t = sb("rope", TILES * 48)
        RO = rope_t[:, :].rearrange("p (i c) -> p i c", c=48)
        qg = sb("q_gain", P)
        kg = sb("k_gain", P)
        g_rows = XR[:, 512:640]
        gcol = sb("gain_columns", 40)
        sk_rows = XR[:, 0:512].rearrange("p (m d) -> p m d", d=P)
        skT_t = sb("subkeys_T", 4 * P)
        skT = skT_t[:, :].rearrange("p (m k) -> p m k", k=P)
        ident = sb("ident", P)
        zeros = sb("zeros", P)
        ones = sb("ones", 1)
        iota16 = sb("iota16", SEL)
        spread = XR[:, 640:880]
        SELW = sb("select_wide", 240)
        SG = sb("select_group", P)
        XS = sb("select_tokens", P)
        QG = sb("group_queries_T", 2 * P)
        S0 = sb("scores", 2 * P)
        S1 = sb("scores_left", 2 * P)
        top = sb("top_values", 32)
        top_i = sb("top_index", 32, U32)
        top_f = sb("top_index_f", 32)
        cand = sb("candidates", 256)
        cand2 = S1
        best = sb("best", SEL)
        pick = sb("pick", SEL, U32)
        pick_a = sb("pick_a", 2 * SEL, U32)
        pick_f = sb("pick_f", 2 * SEL)
        OH = sb("one_hot", 2 * 256)
        id_f = sb("id_f", 3 * SEL)
        IDU = [sb(f"ids_u{p}", SEL, U32) for p in range(2)]
        IDV = [sb(f"ids_v{p}", SEL, U32) for p in range(2)]
        nb0 = sb("minus_best", 1)
        GE = sb("gate_exp", SEL)
        GS = sb("gate_sum", 2)
        GA = [sb(f"gates{p}", SEL) for p in range(2)]
        DOT = sb("dots", SEL)
        GL = sb("gelu", SEL)
        AV = sb("activations", SEL)
        SSQ = sb("sum_squares", 11)
        MS = sb("mean_squares", 11)
        RT = sb("roots", 11)
        RS = sb("rstd", 11)
        nt_ = sb("newton", 1)
        hs = sb("head_sums", 40)
        red = sb("reductions", 16)
        m8 = sb("max8", 8)

        s_x = [sem(f"s_x{i}") for i in range(TILES)]
        s_small = sem("s_small")
        s_rope = sem("s_rope")
        s_win = [sem(f"s_win{c}") for c in range(KC)]
        s_wb = [sem(f"s_wb{k}") for k in range(WB)]
        s_wbu = sem("s_wbu")
        s_ev = sem("s_ev")
        s_grow = sem("s_grow")
        s_const = sem("s_const")
        s_constp = sem("s_constp")
        s_tr = sem("s_tr")
        s_setup = sem("s_setup")
        s_ssq = sem("s_ssq")
        s_ms = sem("s_ms")
        s_root = sem("s_root")
        s_rstd = sem("s_rstd")
        s_xh = sem("s_xh")
        s_xhT = sem("s_xhT")
        s_xT = sem("s_xT")
        s_proj = sem("s_proj")
        s_pj = sem("s_pj")
        s_pjd = sem("s_pjd")
        s_hms = sem("s_hms")
        s_hroot = sem("s_hroot")
        s_roped = sem("s_roped")
        s_qkT = sem("s_qkT")
        s_qk = sem("s_qk")
        s_qkd = sem("s_qkd")
        s_idx = sem("s_idx")
        s_relu = sem("s_relu")
        s_logit = sem("s_logit")
        s_zread = sem("s_zread")
        s_e1 = sem("s_e1")
        s_e2 = sem("s_e2")
        s_e3 = sem("s_e3")
        s_prob = sem("s_prob")
        s_probb = sem("s_probb")
        s_PTp = sem("s_PTp")
        s_PT = sem("s_PT")
        s_PTd = sem("s_PTd")
        s_pv = sem("s_pv")
        s_oT = sem("s_oT")
        s_wo = sem("s_wo")
        s_res = sem("s_res")
        s_ld = [sem(f"s_ld{k}") for k in range(16)]
        s_QG = sem("s_QG")
        s_XS = sem("s_XS")
        s_xr = sem("s_xr")
        s_xru = sem("s_xru")
        s_s = sem("s_s")
        s_S = sem("s_S")
        s_best = sem("s_best")
        s_gexp = sem("s_gexp")
        s_IDU = sem("s_IDU")
        s_IDV = sem("s_IDV")
        s_dots = sem("s_dots")
        s_gelu = sem("s_gelu")
        s_act = sem("s_act")
        s_DG = sem("s_DG")
        s_vused = sem("s_vused")
        s_fin = sem("s_fin")
        s_out = sem("s_out")
        s_dve = sem("s_dve")
        s_actc = sem("s_actc")
        s_carry = sem("s_carry")

        NORM = {("a", 1): 0, ("a", 0): 1, ("a", 2): 2, ("f0", 1): 3, ("f0", 0): 4, ("f0", 2): 5,
                ("b", 0): 6, ("b", 1): 7, ("f1", 1): 8, ("b", 2): 9, ("f1", 2): 10}
        XTC = [2, 4, 6, 8, 10, 12, 14, 18, 20, 24, 26]
        GAIN = {"a": 0, "kv": 1, "b": 2, "f0": 3, "f1": 4}
        PROJ = {1: 0, 0: 1, 2: 2}
        ATT = {(0, 1): 0, (0, 0): 1, (0, 2): 2, (1, 1): 3, (1, 2): 4}
        STEPS = {(0, 1): 0, (0, 2): 24, (1, 1): 48, (1, 2): 84}
        STREAM = ([("a_wo", m) for m in range(8)] + [("pq0", m) for m in range(16)]) * 2 + \
                 ([("kv", m) for m in range(4)] + [("b_wq", m) for m in range(8)] +
                  [("b_wo", m) for m in range(8)] + [("pq1", m) for m in range(16)]) * 2
        EV = [sum(k not in ("a_wo", "b_wo") for k, _ in STREAM[:b]) for b in range(len(STREAM) + 1)]
        WO_CHUNK = {(0, 1): 0, (0, 2): 2, (1, 1): 4, (1, 2): 6}
        PBANK = [4, 0, 4]
        PTB = [0, 4, 5]
        PTD = {(0, 1): 0, (0, 2): 2, (1, 1): 4, (1, 2): 6}
        LOOPED = (1, 2)
        FIN = {(0, 1): 1, (0, 0): 2, (0, 2): 3, (1, 1): 4, (1, 2): 5}

        def first_block(l, i, kind):
            at = {"wo": 0, "pq": 8} if l == 0 else {"kv": 0, "bq": 4, "wo": 12, "pq": 20}
            return STEPS[l, i] + at[kind]

        def group_no(l, i, j):
            return {(0, 1): 0, (0, 0): 8, (0, 2): 9, (1, 1): 17, (1, 2): 25}[l, i] + j

        def group_at(i, j):
            return {1: 0, 0: 8, 2: 9}[i] + j

        early = {(0, 1, 0): [("qkv", 2)],
                 (0, 1, 1): [("half", 0, 0, 0), ("half", 0, 0, 1)],
                 (0, 1, 2): [("select", 2)],
                 (0, 1, 3): [("half", 0, 2, 0)],
                 (0, 1, 4): [("half", 0, 2, 1)],
                 (0, 1, 5): [("wo", 0, 2, 1)],
                 (0, 1, 6): [("pq", 0, 2, 0, 5)],
                 (0, 1, 7): [("pq", 0, 2, 10, 16)],
                 (0, 2, 1): [("norm", "b", 0), ("norm", "b", 1)],
                 (0, 2, 2): [("bq", 1, 0, 4)],
                 (0, 2, 3): [("half", 1, 1, 0)],
                 (0, 2, 4): [("half", 1, 1, 1)],
                 (0, 2, 5): [("wo", 1, 1, 1)],
                 (0, 2, 6): [("pq", 1, 1, 0, 5)],
                 (0, 2, 7): [("pq", 1, 1, 10, 16)],
                 (1, 1, 1): [("norm", "b", 2)],
                 (1, 1, 2): [("bq", 2, 0, 4)],
                 (1, 1, 3): [("half", 1, 2, 0)],
                 (1, 1, 4): [("half", 1, 2, 1)],
                 (1, 1, 5): [("wo", 1, 2, 1)],
                 (1, 1, 6): [("pq", 1, 2, 0, 5)],
                 (1, 1, 7): [("pq", 1, 2, 10, 16)]}
        late = {(0, 1, 4): [("wo", 0, 2, 0)],
                (0, 1, 5): [("norm", "f0", 0), ("norm", "f0", 2)],
                (0, 1, 6): [("pq", 0, 2, 5, 10)],
                (0, 2, 1): [("kv", 1)],
                (0, 2, 2): [("bq", 1, 4, 8)],
                (0, 2, 4): [("wo", 1, 1, 0)],
                (0, 2, 5): [("norm", "f1", 1)],
                (0, 2, 6): [("pq", 1, 1, 5, 10)],
                (1, 1, 1): [("kv", 2)],
                (1, 1, 2): [("bq", 2, 4, 8)],
                (1, 1, 4): [("wo", 1, 2, 0)],
                (1, 1, 5): [("norm", "f1", 2)],
                (1, 1, 6): [("pq", 1, 2, 5, 10)]}
        ORDER = [(0, 1), (0, 0), (0, 2), (1, 1), (1, 2)]
        GROUPS = [(l, i, j) for l, i in ORDER for j in range(8 if i else 1)]
        EARLY, ROUTE, LATE = 2, 7, 12
        RING = 8

        def before(l, i, j):
            if not number(j):
                return l, i, j - 1
            n = group_no(l, i, j)
            return GROUPS[n - 1] if n else None

        def after(l, i, j):
            if not number(j):
                return l, i, j + 1
            n = group_no(l, i, j)
            return GROUPS[n + 1] if n + 1 < len(GROUPS) else None

        def number(n):
            return isinstance(n, int)

        def ends(l, i, j):
            return number(j) and j == (7 if i else 0)

        def walk(eng, step, chain=None, per=0):
            for l, i in ORDER:
                if (l, i) != LOOPED:
                    for j in range(8 if i else 1):
                        step(l, i, j, group_no(l, i, j) % 2)
                    continue
                step(l, i, 0, group_no(l, i, 0) % 2)
                start = chain.n if chain else 0
                with eng.Fori(0, 3) as t:
                    if chain:
                        chain.off = t * (2 * per)
                    for q in (1, 2):
                        step(l, i, 2 * t + q, (group_no(l, i, 0) + q) % 2)
                if chain:
                    assert chain.n - start == 2 * per, (chain.n - start, per)
                    chain.n, chain.off = start + 6 * per, 0
                step(l, i, 7, group_no(l, i, 7) % 2)

        def gaps(steps, where, l, i, j):
            if isinstance(j, int):
                for name, *what in where.get((l, i, j), ()):
                    if name in steps:
                        steps[name](*what)

        block = ctx.enter_context(nc.Block())

        @block.sync
        def _(sp):
            sp.dma_start(hx[:, 1, :], x[0, 0:P, :]).then_inc(s_x[1], 16)
            sp.dma_start(hx[:META, 0, :], meta).then_inc(s_x[0], 16)
            for n, g in enumerate((a_norm[0], kv_norm, b_norm[0], ffn_norm[0], ffn_norm[1])):
                sp.dma_start(g_rows[8 * n:8 * n + 8, :], g.rearrange("(c p) -> c p", p=P)).then_inc(s_small, 16)
            sp.dma_start(sk_rows, peer_subkeys.rearrange("l c k d -> k (l c) d")).then_inc(s_small, 16)
            w_rows = a_w_in[0].rearrange("(c p) n -> p c n", p=P)
            for c in range(KC):
                sp.dma_start(w_in[:, c, :], w_rows[:, c, :]).then_inc(s_win[c], 16)
                if c == 0:
                    sp.dma_start(hx[:, 2, :], x[0, P:2 * P, :]).then_inc(s_x[2], 16)
                if c == 1:
                    sp.dma_start(RO[:META, 0, :], rope[0:META, :]).then_inc(s_rope, 16)
                    sp.dma_start(RO[:, 1:3, :], rope[META:T, :].rearrange("(i p) c -> p i c", p=P)).then_inc(s_rope, 16)
                    sp.dma_start(qg[:, :], a_q_norm.broadcast_to([P, P])).then_inc(s_rope, 16)
                    sp.dma_start(kg[:, :], a_k_norm.broadcast_to([P, P])).then_inc(s_rope, 16)
            for l in range(2):
                sp.dma_start(grow[l][:, :], ffn_norm[l:l + 1].broadcast_to([P, D])).then_inc(s_grow, 16)
            rows = {"a_wo": a_w_o[0], "b_wo": b_w_o[0], "pq0": peer_w_q[0], "pq1": peer_w_q[1], "kv": kv_w,
                    "b_wq": b_w_q[0]}
            rows = {k: w.rearrange("(c p) n -> p c n", p=P) for k, w in rows.items()}
            stored = 0
            for b, (kind, m) in enumerate(STREAM):
                if b >= WB:
                    sp.wait_ge(s_wbu, b - WB + 1)
                sp.dma_start(wb[:, b % WB, :, :], rows[kind][:, :, P * m:P * m + P]).then_inc(s_wb[b % WB], 16)
            for i in (1, 2):
                sp.wait_ge(s_fin, FIN[1, i])
                sp.dma_start(out[0, (i - 1) * P:i * P, :], hx[:, i, :]).then_inc(s_out, 16)
            sp.wait_ge(s_out, 32)

        @block.gpsimd
        def _(pool):
            pool.memset(ident[:, :], 0.0)
            pool.memset(spread, 0.0)
            pool.memset(zeros[:, :], 0.0)
            pool.memset(ones[:, :], 1.0)
            pool.memset(l_t[:, :], 0.0)
            pool.memset(BIAS[:, :], 0.0)
            pool.memset(LATER[:, :], -MASKED)
            pool.iota(iota16[:, :], pattern=[[1, SEL]], base=0, channel_multiplier=0,
                      allow_small_or_imprecise_dtypes=True).then_inc(s_constp, 1)
            pool.wait_ge(s_constp, 1)
            pool.affine_select(out=ident[:, :], in_=ident[:, :], compare_op=ALU.not_equal, fill=1.0, base=0,
                               pattern=[[-1, P]], channel_multiplier=1).then_inc(s_constp, 1)
            pool.wait_ge(s_constp, 2)
            pool.tensor_copy(XS[:GT, :].rearrange("p (h t) -> p h t", t=GT),
                             ident[:GT, :GT].unsqueeze(1).broadcast_to([GT, HEADS, GT]))
            pool.affine_select(out=spread[:GT, :], in_=spread[:GT, :], compare_op=ALU.not_equal, fill=1.0,
                               base=112, pattern=[[-1, 240]], channel_multiplier=1)
            pool.affine_select(out=LATER[:, :], in_=LATER[:, :], compare_op=ALU.is_ge, fill=MASKED,
                               base=P + META, pattern=[[-1, T + 1]], channel_multiplier=1)
            pool.affine_select(out=BIAS[:META, T - META:], in_=BIAS[:META, T - META:], compare_op=ALU.is_ge,
                               fill=NEG, base=0, pattern=[[-1, META]], channel_multiplier=1).then_inc(s_const, 1)

            def gather(table, ids, k, slot):
                pool.indirect_dma_start(
                    out=ring[:, slot, :], out_offset=None, in_=table,
                    in_offset=bass.IndirectOffsetOnAxis(ap=ids[:, k:k + 1], axis=0)).then_inc(s_ld[slot], 16)

            def carry(n):
                if not number(n):
                    pool.sem_inc(s_carry, 1)

            def u_rows_of(n, par, k):
                if k == 0:
                    pool.wait_ge(s_IDU, n + 1)
                    carry(n)
                    if number(n) and n == 0:
                        pool.wait_ge(s_proj, 3)
                if k % 4 == 0 and not (number(n) and 16 * n + k <= 4):
                    pool.wait_ge(s_dots, 16 * n + k + 4 - RING)
                    carry(n)
                gather(u_rows, IDU[par], k, k % RING)

            def v_rows_of(n, par, k):
                if k == 0:
                    pool.wait_ge(s_IDV, n + 1)
                    carry(n)
                if k % 4 == 0 and not (number(n) and 16 * n + k <= 4):
                    pool.wait_ge(s_vused, 16 * n + k + 4 - RING)
                    carry(n)
                gather(v_rows, IDV[par], k, RING + k % RING)

            def step(l, i, j, par):
                n = group_no(l, i, j)
                for k in range(16):
                    u_rows_of(n, par, k)
                    if not (number(n) and n == 0):
                        v_rows_of(n - 1, 1 - par, k)

            walk(pool, step)
            for k in range(16):
                v_rows_of(len(GROUPS) - 1, (len(GROUPS) - 1) % 2, k)

        @block.scalar
        def _(act):
            c = Chain(act, s_actc)
            A = act.activation

            def norm(kind, i):
                k, n = NORM[kind, i], NT[i]
                if k:
                    act.wait_ge(s_xhT, 2 * k)
                if kind == "a":
                    act.wait_ge(s_x[i], 16)
                elif kind == "b":
                    act.wait_ge(s_fin, FIN[0, i])
                elif i:
                    act.wait_ge(s_res, WO_CHUNK[0 if kind == "f0" else 1, i] + 2)
                A(XH[:n, :], hx[:n, i, :], ACT.Square, accum_out=SSQ[:n, k:k + 1]).then_inc(s_ssq, 1)
                act.wait_ge(s_ms, k + 1)
                A(RT[:n, k:k + 1], MS[:n, k:k + 1], ACT.Sqrt).then_inc(s_root, 1)
                act.wait_ge(s_rstd, k + 1)
                A(XH[:n, :], hx[:n, i, :], ACT.Copy, scale=RS[:n, k:k + 1]).then_inc(s_xh, 1)

            def project(i):
                n, b, p = NT[i], PBANK[i], PROJ[i]
                act.wait_ge(s_proj, p + 1)
                A(PJ[i][:n, 0:8, :], bank[:n, b:b + 2, :].rearrange("p b (h d) -> p (b h) d", d=P), ACT.Copy)
                A(PJt[i][:n, 12 * P:12 * P + 320], bank[:n, b + 3, 0:320], ACT.Copy)
                A(WI[:n, i, :], bank[:n, b + 3, 320:324], ACT.Copy).then_inc(s_pj, 1)

            def qkv(i):
                n, p = NT[i], PROJ[i]
                act.wait_ge(s_hms, p + 1)
                A(hs[:n, 20:30], hs[:n, 0:10], ACT.Sqrt).then_inc(s_hroot, 1)
                act.wait_ge(s_qkT, p + 1)
                src = bank[:, 0:2, :].rearrange("p b (h n) -> p (b h) n", n=n) if n == P else \
                    bank[:, 0, :8 * n].rearrange("p (h n) -> p h n", n=n)
                A(qT[i][:, :, :], src, ACT.Copy).then_inc(s_qk, 1)

            def select(i):
                n = NT[i]
                act.wait_ge(s_idx, i)
                A(R4[:n, :, :KEYS[i]], bank[:n, 0:4, :KEYS[i]], ACT.Relu, scale=IDX_SCALE).then_inc(s_relu, 1)

            def half(l, i, g):
                n, keys, t = NT[i], KEYS[i], ATT[l, i]
                u = 2 * t + g
                act.wait_ge(s_e1, u + 1)
                if l == 0:
                    A(L[:n, :, :keys], L[:n, :, :keys], ACT.Exp).then_inc(s_e2, 1)
                else:
                    c.do(A(E4[:n, :, :keys], E4[:n, :, :keys], ACT.Exp, scale=-1.0))
                    A(E4[:n, :, :keys], E4[:n, :, :keys], ACT.Ln, bias=1.0).then_inc(s_e2, 1)
                    act.wait_ge(s_e3, u - 6 + 1)
                    A(L[:n, :, :keys], L[:n, :, :keys], ACT.Exp).then_inc(s_probb, 1)
                act.wait_ge(s_PTp, u + 1)
                kn = NT[i]
                A(PT[:kn, i, :GROUP * n], bank[:kn, PTB[i], :GROUP * n], ACT.Copy).then_inc(s_PT, 1)
                act.wait_ge(s_pv, u + 1)
                A(oT[i][:, GROUP * g:GROUP * (g + 1), :],
                  bank[:, 3, :GROUP * n].rearrange("p (h n) -> p h n", n=n), ACT.Copy).then_inc(s_oT, 1)

            def copied(b, dst, src):
                act.wait_ge(s_wbu, b + 1)
                return A(dst, src, ACT.Copy)

            def pq(l, i, m0, m1):
                for m in range(m0, m1):
                    b = first_block(l, i, "pq") + m
                    with_0 = l == 0 and i == 2
                    g0, g1 = (8 if with_0 else group_at(i, 0)), group_at(i, 0) + 8
                    w = GT * (g1 - g0)
                    copied(b, QTw[:, m % 2, g0:g1, m // 2, :],
                           bank[:, 3 + EV[b] % 3, :w].rearrange("p (g t) -> p g t", t=GT)).then_inc(s_ev, 1)

            def kv(i):
                for m in range(4):
                    b = first_block(1, i, "kv") + m
                    k = 3 + EV[b] % 3
                    if m < 2:
                        a, w = (0, META + P) if i == 1 else (META + P, P)
                        copied(b, kT[:, m, a:a + w], bank[:, k, :w]).then_inc(s_ev, 1)
                    else:
                        d = slice(P * (m - 2), P * (m - 1))
                        if i == 1:
                            copied(b, V[:META, 0, d], bank[:META, k, P:2 * P])
                        copied(b, V[:, i, d], bank[:, k, :P]).then_inc(s_ev, 1)

            def bq(i, m0, m1):
                for m in range(m0, m1):
                    b = first_block(1, i, "bq") + m
                    copied(b, qT[i][:, m, :], bank[:, 3 + EV[b] % 3, :P]).then_inc(s_ev, 1)

            gap = {"norm": norm, "qkv": qkv, "select": select, "half": half, "pq": pq, "kv": kv, "bq": bq}

            act.wait_ge(s_const, 1)
            for i in (1, 0, 2):
                norm("a", i)
            project(1)
            qkv(1)
            project(0)
            qkv(0)
            select(1)
            project(2)
            half(0, 1, 0)
            half(0, 1, 1)
            norm("f0", 1)
            pq(0, 1, 0, 16)
            act.wait_ge(s_ev, 16)

            def route(l, i, j):
                n = group_no(l, i, j)
                first = number(n) and n == 0

                def carry():
                    if not number(n):
                        act.sem_inc(s_carry, 1)

                r = NORM[("f0", "f1")[l], i]
                nt = NT[i]
                g = group_at(i, j)
                if not first:
                    act.wait_ge(s_s, n)
                    carry()
                if number(j) and j == 0:
                    act.wait_ge(s_ev, EV[first_block(l, i or 2, "pq") + 16])
                A(QG[:, :].rearrange("p (c m) -> p c m", c=2), QT[:, :, bass.ds(g, 1), :].rearrange("p c o m -> p c (o m)"),
                  ACT.Copy).then_inc(s_QG, 1)
                if not first:
                    act.wait_ge(s_xr, n)
                    carry()
                A(XS[:nt, :].rearrange("p (h t) -> p h t", t=GT),
                  ident[:nt, bass.ds(16 * j, 16)].unsqueeze(1).broadcast_to([nt, HEADS, GT]),
                  ACT.Copy, scale=RS[:nt, r:r + 1]).then_inc(s_XS, 1)
                if not first:
                    act.wait_ge(s_IDU, n)
                act.wait_ge(s_s, n + 1)
                A(S0[:, :], bank[:, 2, 0:2 * P], ACT.Copy).then_inc(s_S, 1)
                act.wait_ge(s_best, n + 1)
                A(GE[:, :], best[:, :], ACT.Exp, bias=nb0[:, :], accum_out=GS[:, 0:1]).then_inc(s_gexp, 1)

            def step(l, i, j, par):
                n = group_no(l, i, j)
                first = number(n) and n == 0

                def carry():
                    if not number(n):
                        act.sem_inc(s_carry, 1)

                gaps(gap, early, l, i, j)
                if after(l, i, j):
                    route(*after(l, i, j))
                gaps(gap, late, l, i, j)
                act.wait_ge(s_dots, 16 * n + 16)
                A(GL[:, :], DOT[:, :], ACT.Gelu).then_inc(s_gelu, 1)
                if not first:
                    act.wait_ge(s_DG, 16 * n)
                    carry()
                c.do(A(SG[:, :], SELW[:, bass.ds(112 - 16 * j, P)], ACT.Copy))
                act.wait_ge(s_act, n + 1)
                if first:
                    act.wait_ge(s_qkT, 3)
                for k in range(16):
                    if not first and k % 4 == 0:
                        act.wait_ge(s_vused, 16 * (n - 1) + k + 4)
                    A(DG[:, k, :], SG[:, :], ACT.Copy, scale=AV[:, k:k + 1]).then_inc(s_DG, 1)

            route(*GROUPS[0])
            walk(act, step, c, 1)

        @block.vector
        def _(dve):
            c = Chain(dve, s_dve)
            tt, ts, stt = dve.tensor_tensor, dve.tensor_scalar, dve.scalar_tensor_tensor

            dve.wait_ge(s_tr, 1)
            dve.tensor_copy(gcol[:, :], bank[:, 0, 0:40])
            dve.tensor_copy(skT[:, :, :], bank[:, 1, :].rearrange("p (m k) -> p m k", k=P))
            dve.tensor_copy(SELW[:, :], bank[:, 2, 0:240]).then_inc(s_setup, 1)
            dve.wait_ge(s_setup, 1)

            def inverse_root(dst, ms, root, tmp):
                c.do(dve.reciprocal(dst, root))
                c.do(tt(tmp, ms, dst, ALU.mult))
                c.do(tt(tmp, tmp, dst, ALU.mult))
                c.do(ts(tmp, tmp, -0.5, 1.5, ALU.mult, ALU.add))
                return tt(dst, dst, tmp, ALU.mult)

            def norm(kind, i):
                k, n = NORM[kind, i], NT[i]
                dve.wait_ge(s_ssq, k + 1)
                ts(MS[:n, k:k + 1], SSQ[:n, k:k + 1], 1.0 / D, EPS, ALU.mult, ALU.add).then_inc(s_ms, 1)
                dve.wait_ge(s_root, k + 1)
                inverse_root(RS[:n, k:k + 1], MS[:n, k:k + 1], RT[:n, k:k + 1], nt_[:n, 0:1]).then_inc(s_rstd, 1)
                o = META if i else 0
                if kind == "a":
                    outs = [("a", xT if i == 1 else xT2)]
                elif kind == "b":
                    outs = [("kv", xT2)] + ([("b", xT)] if i else [])
                else:
                    outs = [(kind, xT)]
                for hf in range(2):
                    dve.wait_ge(s_xhT, 2 * k + hf + 1)
                    src = bank[:, 4 + hf, :4 * n].rearrange("p (c n) -> p c n", n=n)
                    for gain, dst in outs:
                        a = GAIN[gain] * 8 + 4 * hf
                        tt(dst[:, 4 * hf:4 * hf + 4, o:o + n], src,
                           gcol[:, a:a + 4].unsqueeze(2).broadcast_to([P, 4, n]), ALU.mult).then_inc(s_xT, 1)

            def rotate(view, i, hd, at, heads):
                n = NT[i]
                cos = RO[:n, i, at:at + hd].unsqueeze(1).broadcast_to([n, heads, hd])
                sin = RO[:n, i, at + hd:at + 2 * hd].unsqueeze(1).broadcast_to([n, heads, hd])
                a, b = view[:, :, 0:hd], view[:, :, hd:2 * hd]
                w = heads * hd
                t = [TMP[:n, m * w:(m + 1) * w].rearrange("p (h d) -> p h d", d=hd) for m in range(4)]
                tt(t[0], a, cos, ALU.mult)
                tt(t[1], b, sin, ALU.mult)
                tt(t[2], b, cos, ALU.mult)
                c.do(tt(t[3], a, sin, ALU.mult))
                tt(a, t[0], t[1], ALU.subtract)
                return tt(b, t[2], t[3], ALU.add)

            def project(i):
                n, b, p = NT[i], PBANK[i], PROJ[i]
                dve.wait_ge(s_proj, p + 1)
                dve.tensor_copy(PJ[i][:n, 8:10, :], bank[:n, b + 2, 0:256].rearrange("p (b d) -> p b d", d=P))
                dve.tensor_copy(V[:n, i, :], bank[:n, b + 2, 256:512]).then_inc(s_pjd, 1)

            def qkv(i):
                n, p = NT[i], PROJ[i]
                dve.wait_ge(s_pjd, p + 1)
                dve.wait_ge(s_pj, p + 1)
                qk = PJ[i][:n, 0:10, :]
                sq = TMP[:n, :].rearrange("p (h d) -> p h d", d=P)
                c.do(tt(sq, qk, qk, ALU.mult))
                c.do(dve.reduce_sum(hs[:n, 0:10], sq, AX.X))
                ts(hs[:n, 0:10], hs[:n, 0:10], 1.0 / P, EPS, ALU.mult, ALU.add).then_inc(s_hms, 1)
                c.do(rotate(PJt[i][:n, 12 * P:12 * P + 320].rearrange("p (h d) -> p h d", d=64), i, 8, 32, 5))
                dve.tensor_copy(PJ[i][:n, 14, 64:128], PJ[i][:n, 14, 0:64])
                dve.wait_ge(s_hroot, p + 1)
                c.do(inverse_root(hs[:n, 10:20], hs[:n, 0:10], hs[:n, 20:30], hs[:n, 30:40]))
                c.do(tt(qk, qk, hs[:n, 10:20].unsqueeze(2).broadcast_to([n, 10, P]), ALU.mult))
                tt(PJ[i][:n, 0:8, :], PJ[i][:n, 0:8, :], qg[:n, :].unsqueeze(1).broadcast_to([n, 8, P]), ALU.mult)
                c.do(tt(PJ[i][:n, 8:10, :], PJ[i][:n, 8:10, :], kg[:n, :].unsqueeze(1).broadcast_to([n, 2, P]), ALU.mult))
                rotate(qk, i, 16, 0, 10).then_inc(s_roped, 1)
                dve.wait_ge(s_qkT, p + 1)
                w = 5 * n
                if n == P:
                    dve.tensor_copy(kT[:, :, OFF[i]:OFF[i] + n], bank[:, 2, 0:256].rearrange("p (h n) -> p h n", n=n))
                    dve.tensor_copy(qiT[i][:, :, :], bank[:, 2, 256:512].rearrange("p (h n) -> p h n", n=n))
                    c.do(dve.tensor_copy(kiT[:, OFF[i]:OFF[i] + n], bank[:, 3, 0:n]))
                else:
                    src = bank[:, 2, :w].rearrange("p (h n) -> p h n", n=n)
                    dve.tensor_copy(kT[:, :, :n], src[:, 0:2, :])
                    c.do(dve.tensor_copy(kiT[:, :n], src[:, 4, :]))
                dve.sem_inc(s_qkd, 1)

            def later(i, strict):
                a = P + META - OFF[i] + strict
                return LATER[:NT[i], a:a + KEYS[i]]

            def select(i):
                n, keys = NT[i], KEYS[i]
                dve.wait_ge(s_relu, i)
                c.do(ts(SC[:n, :keys], R4[:n, 0, :keys], WI[:n, i, 0:1], None, ALU.mult))
                for h in range(1, IDX_HEADS):
                    c.do(stt(SC[:n, :keys], R4[:n, h, :keys], WI[:n, i, h:h + 1], SC[:n, :keys], ALU.mult, ALU.add))
                c.do(tt(SC[:n, :keys], SC[:n, :keys], later(i, 0), ALU.min))
                src = SC
                for r in range(TOPK // 8):
                    c.do(dve.max(m8[:n, :], src[:n, :keys]))
                    dst = WK if r % 2 == 0 else SC
                    c.do(dve.match_replace(dst[:n, :keys], m8[:n, :], src[:n, :keys], TAKEN))
                    src = dst
                c.do(ts(BIAS[:n, :keys], src[:n, :keys], TAKEN_BELOW, NEG, ALU.is_gt, ALU.mult))
                c.do(tt(BIAS[:n, :keys], BIAS[:n, :keys], later(i, 0), ALU.min))

            def heads_out(i, u):
                n = NT[i]
                if i:
                    dve.wait_ge(s_PTp, u + 1)
                    for j in range(i):
                        kn = NT[j]
                        ins = dve.tensor_copy(PT[:kn, j, :GROUP * n], bank[:kn, PTB[j], :GROUP * n])
                    ins.then_inc(s_PTd, 1)

            def half(l, i, g):
                n, keys = NT[i], KEYS[i]
                u = 2 * ATT[l, i] + g
                z, e, cs = L[:n, :, :keys], E4[:n, :, :keys], C4[:n, :, :keys]
                dve.wait_ge(s_logit, u + 1)
                if l == 0:
                    a = 0 if i else T - META
                    stt(z, bank[:n, 0:4, :keys], SCALE, BIAS[:n, a:a + keys].unsqueeze(1).broadcast_to([n, GROUP, keys]),
                        ALU.mult, ALU.add).then_inc(s_zread, 1)
                    dve.wait_ge(s_zread, u + 1)
                    c.do(dve.reduce_max(red[:n, 0:4], z, AX.X))
                    tt(z, z, red[:n, 0:4].unsqueeze(2).broadcast_to([n, GROUP, keys]), ALU.subtract).then_inc(s_e1, 1)
                    dve.wait_ge(s_e2, u + 1)
                    c.do(dve.reduce_sum(red[:n, 4:8], z, AX.X))
                    c.do(dve.reciprocal(red[:n, 8:12], red[:n, 4:8]))
                    tt(z, z, red[:n, 8:12].unsqueeze(2).broadcast_to([n, GROUP, keys]), ALU.mult).then_inc(s_prob, 1)
                else:
                    ts(z, bank[:n, 0:4, :keys], SCALE, None, ALU.mult).then_inc(s_zread, 1)
                    dve.wait_ge(s_zread, u + 1)
                    stt(e, z, -1.0, z, ALU.mult, ALU.max).then_inc(s_e1, 1)
                    dve.wait_ge(s_e2, u + 1)
                    c.do(stt(e, z, 0.0, e, ALU.max, ALU.add))
                    mask = later(i, 1).unsqueeze(1).broadcast_to([n, GROUP, keys])
                    c.do(stt(e, mask, 0.0, e, ALU.is_gt, ALU.mult))
                    for h in range(GROUP):
                        ins = dve.tensor_tensor_scan(C4[:n, h, 0:keys][:, ::-1], ones[:n, :].broadcast_to([n, keys]),
                                                     E4[:n, h, 0:keys][:, ::-1], 0.0, ALU.mult, ALU.add)
                    c.do(ins)
                    c.do(tt(z, z, cs, ALU.subtract))
                    tt(z, z, mask, ALU.min).then_inc(s_e3, 1)
                heads_out(i, u)

            def wo(l, i, m):
                q = WO_CHUNK[l, i] + m
                dve.wait_ge(s_wo, q + 1)
                d = slice(512 * m, 512 * m + 512)
                if (l, i) == (0, 2):
                    tt(hx[:META, 0, d], hx[:META, 0, d], bank[:META, 4, :], ALU.add)
                tt(hx[:, i, d], hx[:, i, d], bank[:, 3 + 2 * m, :], ALU.add).then_inc(s_res, 1)

            gap = {"norm": norm, "qkv": qkv, "select": select, "half": half, "wo": wo}

            norm("a", 1)
            norm("a", 0)
            norm("a", 2)
            dve.wait_ge(s_rope, 64)
            project(1)
            qkv(1)
            project(0)
            qkv(0)
            select(1)
            project(2)
            half(0, 1, 0)
            half(0, 1, 1)
            wo(0, 1, 0)
            wo(0, 1, 1)
            norm("f0", 1)
            dve.wait_ge(s_grow, 32)

            def route(l, i, j, par):
                n = group_no(l, i, j)

                def carry():
                    if not number(n):
                        dve.sem_inc(s_carry, 1)

                dve.wait_ge(s_S, n + 1)
                carry()
                for h in range(2):
                    s = slice(P * h, P * h + P)
                    ins = dve.max(top[:, 16 * h:16 * h + 8], S0[:, s])
                c.do(ins)
                carry()
                for h in range(2):
                    s, t = slice(P * h, P * h + P), slice(16 * h, 16 * h + 8)
                    dve.max_index(top_i[:, t], top[:, t], S0[:, s])
                    ins = dve.match_replace(S1[:, s], top[:, t], S0[:, s], TAKEN)
                c.do(ins)
                carry()
                for h in range(2):
                    s = slice(P * h, P * h + P)
                    ins = dve.max(top[:, 16 * h + 8:16 * h + 16], S1[:, s])
                c.do(ins)
                carry()
                for h in range(2):
                    s, t = slice(P * h, P * h + P), slice(16 * h + 8, 16 * h + 16)
                    dve.max_index(top_i[:, t], top[:, t], S1[:, s])
                a = top[:, 0:16].unsqueeze(2).broadcast_to([P, 16, 16])
                b = top[:, 16:32].unsqueeze(1).broadcast_to([P, 16, 16])
                c.do(tt(cand[:, :].rearrange("p (a b) -> p a b", b=16), a, b, ALU.add))
                carry()
                c.do(dve.max(best[:, 0:8], cand[:, :]))
                carry()
                dve.max_index(pick[:, 0:8], best[:, 0:8], cand[:, :])
                c.do(dve.match_replace(cand2[:, :], best[:, 0:8], cand[:, :], TAKEN))
                carry()
                c.do(dve.max(best[:, 8:16], cand2[:, :]))
                carry()
                dve.max_index(pick[:, 8:16], best[:, 8:16], cand2[:, :])
                ts(nb0[:, :], best[:, 0:1], -1.0, None, ALU.mult).then_inc(s_best, 1)
                dve.wait_ge(s_best, n + 1)
                ts(pick_a[:, 0:16], pick[:, :], 4, None, ALU.logical_shift_right)
                ts(pick_a[:, 16:32], pick[:, :], 15, None, ALU.bitwise_and)
                c.do(dve.tensor_copy(top_f[:, :], top_i[:, :]))
                c.do(dve.tensor_copy(pick_f[:, :], pick_a[:, :]))
                oh = OH[:, :].rearrange("p (k a) -> p k a", a=16)
                c.do(tt(oh, pick_f[:, :].unsqueeze(2).broadcast_to([P, 32, 16]),
                        iota16[:, :].unsqueeze(1).broadcast_to([P, 32, 16]), ALU.is_equal))
                for h in range(2):
                    ins = tt(oh[:, 16 * h:16 * h + 16, :], oh[:, 16 * h:16 * h + 16, :],
                             top_f[:, 16 * h:16 * h + 16].unsqueeze(1).broadcast_to([P, 16, 16]), ALU.mult)
                c.do(ins)
                c.do(dve.reduce_sum(id_f[:, 0:32], oh, AX.X))
                c.do(stt(id_f[:, 32:48], id_f[:, 0:16], float(NKEYS), id_f[:, 16:32], ALU.mult, ALU.add))
                ts(IDU[par][:, :], id_f[:, 32:48], float(EXPERTS * l), None, ALU.add).then_inc(s_IDU, 1)
                dve.wait_ge(s_gexp, n + 1)
                c.do(dve.reciprocal(GS[:, 1:2], GS[:, 0:1]))
                c.do(ts(GA[par][:, :], GE[:, :], GS[:, 1:2], None, ALU.mult))

            def step(l, i, j, par):
                n = group_no(l, i, j)
                first = number(n) and n == 0
                dve.wait_ge(s_xr, n + 1)
                tt(XR[:, :], bank[:, 0:2, :].rearrange("p b n -> p (b n)"), grow[l][:, :], ALU.mult).then_inc(s_xru, 1)
                dve.wait_ge(s_xru, n + 1)
                for k in range(16):
                    slot = k % RING
                    dve.wait_ge(s_ld[slot], 16 * (2 * n + k // RING + 1))
                    stt(ring[:, slot, :], ring[:, slot, :], 1.0, XR[:, :], ALU.mult, ALU.mult,
                        accum_out=DOT[:, k:k + 1]).then_inc(s_dots, 1)
                    if k == EARLY:
                        gaps(gap, early, l, i, j)
                    if k == ROUTE:
                        if not (number(n) and n < 2):
                            dve.wait_ge(s_vused, 16 * (n - 1))
                        dve.wait_ge(s_IDU, n + 1)
                        dve.tensor_copy(IDV[par][:, :], IDU[par][:, :]).then_inc(s_IDV, 1)
                        dve.wait_ge(s_IDV, n + 1)
                        if after(l, i, j):
                            route(*after(l, i, j), 1 - par)
                    if k == LATE:
                        gaps(gap, late, l, i, j)
                dve.wait_ge(s_gelu, n + 1)
                if not first:
                    dve.wait_ge(s_DG, 16 * n)
                tt(AV[:, :], GL[:, :], GA[par][:, :], ALU.mult).then_inc(s_act, 1)
                dve.wait_ge(s_act, n + 1)
                last = before(l, i, j)
                if last and ends(*last):
                    fin(*last)

            def fin(l, i, j):
                n = NT[i]
                dve.wait_ge(s_vused, 16 * (group_no(l, i, j) + 1))
                tt(hx[:n, i, :], hx[:n, i, :], bank[:n, 6:8, :].rearrange("p b n -> p (b n)"), ALU.add).then_inc(s_fin, 1)

            route(*GROUPS[0], 0)
            walk(dve, step, c, UP_STEPS)
            fin(*GROUPS[-1])

        @block.tensor
        def _(pe):
            mm = pe.matmul

            def put(dst, src):
                return pe.transpose(dst, src, ident[:src.shape[0], :src.shape[0]])

            pe.wait_ge(s_const, 1)
            pe.wait_ge(s_small, 96)
            put(bank[:, 0, 0:40], g_rows[:40, :])
            for m in range(4):
                put(bank[:, 1, P * m:P * m + P], sk_rows[:, m, :])
            mm(bank[:, 2, 0:240], XS[:GT, :], spread[:GT, :], start=True, stop=True).then_inc(s_tr, 1)

            def norm(kind, i):
                k, n = NORM[kind, i], NT[i]
                pe.wait_ge(s_xh, k + 1)
                for hf in range(2):
                    if k:
                        pe.wait_ge(s_xT, XTC[k - 1])
                    for m in range(4):
                        cc = 4 * hf + m
                        ins = put(bank[:, 4 + hf, m * n:m * n + n], XH[:n, P * cc:P * cc + P])
                    ins.then_inc(s_xhT, 1)

            def project(i):
                n, b = NT[i], PBANK[i]
                src = xT if i == 1 else xT2
                o = META if i else 0
                pe.wait_ge(s_xT, XTC[NORM["a", i]])
                for cc in range(KC):
                    if i == 1:
                        pe.wait_ge(s_win[cc], 16)
                    for m in range(4):
                        w = min(512, A_COLS - 512 * m)
                        ins = mm(bank[:n, b + m, :w], src[:, cc, o:o + n], w_in[:, cc, 512 * m:512 * m + w],
                                 start=cc == 0, stop=cc == KC - 1)
                ins.then_inc(s_proj, 1)

            def qkv(i):
                n, p = NT[i], PROJ[i]
                pe.wait_ge(s_roped, p + 1)
                for h in range(8):
                    a = h * n
                    put(bank[:, a // 512, a % 512:a % 512 + n], PJ[i][:n, h, :])
                for m, b in enumerate((8, 9, 12, 13, 14)):
                    a = m * n
                    ins = put(bank[:, 2 + a // 512, a % 512:a % 512 + n], PJ[i][:n, b, :])
                ins.then_inc(s_qkT, 1)
                pe.wait_ge(s_qk, p + 1)
                pe.wait_ge(s_qkd, p + 1)

            def select(i):
                n = NT[i]
                for h in range(IDX_HEADS):
                    r = slice(64 * (h % 2), 64 * (h % 2) + 64)
                    ins = mm(bank[:n, h, :KEYS[i]], qiT[i][r, h // 2, :], kiT[r, :KEYS[i]], start=True, stop=True)
                ins.then_inc(s_idx, 1)
                pe.wait_ge(s_relu, i)

            def half(l, i, g):
                n, keys, t = NT[i], KEYS[i], ATT[l, i]
                u = 2 * t + g
                if l == 1 and g == 0:
                    pe.wait_ge(s_ev, EV[first_block(1, i, "wo")])
                for h in range(GROUP):
                    ins = mm(bank[:n, h, :keys], qT[i][:, GROUP * g + h, :], kT[:, g, :keys], start=True, stop=True)
                ins.then_inc(s_logit, 1)
                if l == 0:
                    pe.wait_ge(s_prob, u + 1)
                else:
                    pe.wait_ge(s_probb, u - 6 + 1)
                for j in range(i + 1):
                    for h in range(GROUP):
                        ins = put(bank[:, PTB[j], h * n:h * n + n], L[:n, h, OFF[j]:OFF[j] + P])
                ins.then_inc(s_PTp, 1)
                pe.wait_ge(s_PT, u + 1)
                if i:
                    pe.wait_ge(s_PTd, PTD[l, i] + g + 1)
                for j in range(i + 1):
                    kn = NT[j]
                    ins = mm(bank[:, 3, :GROUP * n], V[:kn, j, P * g:P * g + P], PT[:kn, j, :GROUP * n],
                             start=j == 0, stop=j == i)
                ins.then_inc(s_pv, 1)
                pe.wait_ge(s_oT, u + 1)

            def weights(b):
                pe.wait_ge(s_wb[b % WB], 16 * (b // WB + 1))
                return wb[:, b % WB, :, :]

            def copies(b):
                e = EV[b]
                if e >= 3:
                    pe.wait_ge(s_ev, e - 2)
                return 3 + e % 3

            def wo(l, i, m):
                if (l, i) == (0, 2) and m:
                    pe.wait_ge(s_res, WO_CHUNK[l, i] + 1)
                for q in range(4):
                    b = first_block(l, i, "wo") + 4 * m + q
                    w = weights(b)
                    d = slice(P * q, P * q + P)
                    for h in range(HEADS):
                        ins = mm(bank[:, 3 + 2 * m, d], oT[i][:, h, :], w[:, h, :], start=h == 0, stop=h == HEADS - 1)
                    if (l, i) == (0, 2):
                        for h in range(HEADS):
                            ins = mm(bank[:META, 4, d], oT[0][:, h, :], w[:, h, :], start=h == 0, stop=h == HEADS - 1)
                    ins.then_inc(s_wbu, 1)
                pe.wait_ge(s_wbu, first_block(l, i, "wo") + 4 * m + 4)
                pe.sem_inc(s_wo, 1)

            def pq(l, i, m0, m1):
                o, w = (0, META + P) if (l, i) == (0, 2) else (META, P)
                if m0 == 0:
                    pe.wait_ge(s_xT, XTC[NORM[("f0", "f1")[l], i]])
                for m in range(m0, m1):
                    b = first_block(l, i, "pq") + m
                    k, ws = copies(b), weights(b)
                    for cc in range(KC):
                        ins = mm(bank[:, k, :w], ws[:, cc, :], xT[:, cc, o:o + w], start=cc == 0, stop=cc == KC - 1)
                    ins.then_inc(s_wbu, 1)

            def kv(i):
                pe.wait_ge(s_xT, XTC[NORM["b", i]])
                o, w = (0, META + P) if i == 1 else (META, P)
                for m in range(4):
                    b = first_block(1, i, "kv") + m
                    k, ws = copies(b), weights(b)
                    if m < 2:
                        for cc in range(KC):
                            ins = mm(bank[:, k, :w], ws[:, cc, :], xT2[:, cc, o:o + w], start=cc == 0, stop=cc == KC - 1)
                    else:
                        for cc in range(KC):
                            ins = mm(bank[:, k, :P], xT2[:, cc, META:META + P], ws[:, cc, :], start=cc == 0,
                                     stop=cc == KC - 1)
                        if i == 1:
                            for cc in range(KC):
                                ins = mm(bank[:META, k, P:2 * P], xT2[:, cc, 0:META], ws[:, cc, :], start=cc == 0,
                                         stop=cc == KC - 1)
                    ins.then_inc(s_wbu, 1)

            def bq(i, m0, m1):
                for m in range(m0, m1):
                    b = first_block(1, i, "bq") + m
                    k, ws = copies(b), weights(b)
                    for cc in range(KC):
                        ins = mm(bank[:, k, :P], ws[:, cc, :], xT[:, cc, META:META + P], start=cc == 0, stop=cc == KC - 1)
                    ins.then_inc(s_wbu, 1)

            gap = {"norm": norm, "qkv": qkv, "select": select, "half": half, "wo": wo, "pq": pq, "kv": kv, "bq": bq}

            pe.wait_ge(s_setup, 1)
            norm("a", 1)
            norm("a", 0)
            norm("a", 2)
            project(1)
            pe.wait_ge(s_xT, XTC[2])
            project(0)
            pe.wait_ge(s_pj, 1)
            pe.wait_ge(s_pjd, 1)
            qkv(1)
            pe.wait_ge(s_pj, 2)
            pe.wait_ge(s_pjd, 2)
            qkv(0)
            select(1)
            project(2)
            half(0, 1, 0)
            half(0, 1, 1)
            wo(0, 1, 0)
            wo(0, 1, 1)
            norm("f0", 1)
            pq(0, 1, 0, 16)

            def route(l, i, j):
                n = group_no(l, i, j)
                nt = NT[i]
                pe.wait_ge(s_XS, n + 1)
                if not (number(n) and n == 0):
                    pe.wait_ge(s_xru, n)
                for m in range(2):
                    ins = mm(bank[:, m, :], XS[:nt, :], hx[:nt, i, 512 * m:512 * m + 512], start=True, stop=True)
                ins.then_inc(s_xr, 1)
                pe.wait_ge(s_QG, n + 1)
                if not (number(n) and n == 0):
                    pe.wait_ge(s_S, n)
                for h in range(2):
                    ins = mm(bank[:, 2, P * h:P * h + P], QG[:, P * h:P * h + P], skT[:, 2 * l + h, :],
                             start=True, stop=True)
                ins.then_inc(s_s, 1)

            def clear(l, i):
                if (l, i) != ORDER[0]:
                    pe.wait_ge(s_fin, FIN[l, i] - 1)
                else:
                    pe.wait_ge(s_pj, 3)
                    pe.wait_ge(s_pjd, 3)
                for m in range(2):
                    mm(bank[:, 6 + m, :].rearrange("p (a b) -> p a b", b=P), zeros[:, :],
                       zeros[:, :].unsqueeze(1).broadcast_to([P, 4, P]), start=True, stop=False,
                       skip_group_check=True)

            def v_sum(n, k):
                slot = RING + k % RING
                pe.wait_ge(s_DG, 16 * n + k + 1)
                pe.wait_ge(s_ld[slot], 16 * (2 * n + k // RING + 1))
                for m in range(2):
                    ins = mm(bank[:, 6 + m, :], DG[:, k, :], ring[:, slot, 512 * m:512 * m + 512],
                             start=False, stop=False, skip_group_check=True)
                ins.then_inc(s_vused, 1)

            def step(l, i, j, par):
                n = group_no(l, i, j)
                last = before(l, i, j)
                for k in range(16):
                    if last:
                        v_sum(n - 1, k)
                    if k == EARLY and number(j) and early.get((l, i, j)):
                        pe.wait_ge(s_xru, n + 1)
                        gaps(gap, early, l, i, j)
                    if k == ROUTE and after(l, i, j):
                        route(*after(l, i, j))
                    if k == LATE:
                        gaps(gap, late, l, i, j)
                if last and ends(*last):
                    clear(l, i)

            route(*GROUPS[0])
            clear(*ORDER[0])
            walk(pe, step)
            for k in range(16):
                v_sum(len(GROUPS) - 1, k)


_INS = ["x", "meta_tokens", "a_norm", "a_w_in", "a_q_norm", "a_k_norm", "a_w_o", "kv_norm", "kv_w", "b_norm",
        "b_w_q", "b_w_o", "ffn_norm", "peer_w_q", "peer_subkeys", "peer_u", "peer_v"]


def _rope_table():
    import numpy as np
    pos = np.arange(T, dtype=np.float32)
    cols = []
    for r in (32, 16):
        inv = np.float32(500000.0) ** (-np.arange(r // 2, dtype=np.float32) * np.float32(2.0) / np.float32(r))
        ang = pos[:, None] * inv[None, :].astype(np.float32)
        cols += [np.cos(ang), np.sin(ang)]
    return np.ascontiguousarray(np.concatenate(cols, axis=1).astype(np.float32))


def kernel(**inputs):
    import numpy as _np
    import concourse.bacc as _bacc
    from concourse import mybir as _mybir
    from concourse.bass_utils import run_bass_kernel_spmd as _run

    nc = _bacc.Bacc("TRN2", target_bir_lowering=False, num_devices=1)
    arrays, args = {}, []
    for name in _INS + ["rope"]:
        a = _rope_table() if name == "rope" else _np.ascontiguousarray(inputs[name])
        arrays[f"in_{name}_dram"] = a
        args.append(nc.dram_tensor(f"in_{name}_dram", a.shape, _mybir.dt.from_np(a.dtype), kind="ExternalInput").ap())
    args.append(nc.dram_tensor("out_0_dram", (1, 2 * P, D), F32, kind="ExternalOutput").ap())
    build(nc, *args)
    r = _run(nc, [arrays], core_ids=[0])
    return r.results[0]["out_0_dram"]
```

```python
from contextlib import ExitStack

import concourse.bass as bass
from concourse import mybir

F32 = mybir.dt.float32
U32 = mybir.dt.uint32
ALU = mybir.AluOpType
ACT = mybir.ActivationFunctionType
AX = mybir.AxisListType

P = 128
D = 1024
KC = D // P
META = 16
TILES = 3
NT = [META, P, P]
OFF = [0, META, META + P]
T = META + 2 * P
KEYS = [META, META + P, T]
HEADS = 8
KV = 2
GROUP = HEADS // KV
IDX_HEADS = 4
TOPK = 64
Q_COLS = HEADS * 128
A_COLS = 1860
EXPERTS = 16384
NKEYS = 128
SEL = 16
GT = 16
SCALE = 128.0 ** -0.5
IDX_SCALE = 1.0 / 16.0
EPS = 1e-6
NEG = -1.0e30
MASKED = -3.0e38
TAKEN = -3.4e38
TAKEN_BELOW = -3.2e38
WB = 6
XC = META + P
UP_STEPS = 15


class Chain:

    def __init__(self, eng, sem):
        self.eng, self.sem, self.n, self.off = eng, sem, 0, 0

    def do(self, ins):
        self.n += 1
        ins.then_inc(self.sem, 1)
        self.eng.wait_ge(self.sem, self.n + self.off)


def build(nc, x, meta, a_norm, a_w_in, a_q_norm, a_k_norm, a_w_o, kv_norm, kv_w, b_norm, b_w_q, b_w_o,
          ffn_norm, peer_w_q, peer_subkeys, peer_u, peer_v, rope, out):
    u_rows = peer_u.rearrange("l e d -> (l e) d")
    v_rows = peer_v.rearrange("l e d -> (l e) d")
    with ExitStack() as ctx:
        def sb(name, cols, dt=F32, rows=P):
            return ctx.enter_context(nc.sbuf_tensor(name, [rows, cols], dt))

        def sem(name):
            return ctx.enter_context(nc.semaphore(name))

        bank = ctx.enter_context(nc.psum_tensor("banks", [P, 8, 512], F32))

        arena = sb("arena", 16 * D)
        ring = arena[:, :].rearrange("p (k d) -> p k d", d=D)
        w_r = arena[:, 0:KC * (A_COLS - Q_COLS)].rearrange("p (c n) -> p c n", n=A_COLS - Q_COLS)
        w_q = arena[:, 8 * D:8 * D + KC * Q_COLS].rearrange("p (c n) -> p c n", n=Q_COLS)
        wb_t = sb("weight_blocks", WB * D)
        wb = wb_t[:, :].rearrange("p (s c n) -> p s c n", s=WB, n=P)

        hx_t = sb("residual", TILES * D)
        hx = hx_t[:, :].rearrange("p (i d) -> p i d", d=D)
        x1_t = sb("x_norm_T", KC * XC)
        xT = x1_t[:, :].rearrange("p (c n) -> p c n", n=XC)
        x2_t = sb("kv_norm_T", KC * XC)
        xT2 = x2_t[:, :].rearrange("p (c n) -> p c n", n=XC)
        qt_t = sb("queries_T", 2 * 17 * P)
        QT = qt_t[:, :].rearrange("p (c g m) -> p c g m", c=2, m=P)
        QTw = qt_t[:, :].rearrange("p (c g h t) -> p c g h t", c=2, h=HEADS, t=GT)
        dg_t = sb("diagonals", 16 * P)
        DG = dg_t[:, :].rearrange("p (k m) -> p k m", m=P)
        l_t = sb("logits", GROUP * T)
        L = l_t[:, :].rearrange("p (h k) -> p h k", k=T)
        re_t = sb("index_scores_and_softplus", 2 * GROUP * T)
        r_t, e_t = re_t[:, 0:GROUP * T], re_t[:, GROUP * T:2 * GROUP * T]
        E4 = e_t.rearrange("p (h k) -> p h k", k=T)
        SC, WK = e_t[:, 0:T], e_t[:, T:2 * T]
        R4 = r_t.rearrange("p (h k) -> p h k", k=T)
        C4 = R4
        q_t = [sb("q_T0", HEADS * META), sb("q_T1", HEADS * P), sb("q_T2", HEADS * P)]
        qT = [a[:, :].rearrange("p (h n) -> p h n", h=HEADS) for a in q_t]
        pt_t = sb("weights_T", 3 * 512)
        PT = pt_t[:, :].rearrange("p (j m) -> p j m", m=512)
        TMP = pt_t[:, 0:1280]
        o_t = [sb("heads_T0", HEADS * META), sb("heads_T", HEADS * P)]
        oT = [a[:, :].rearrange("p (h n) -> p h n", h=HEADS) for a in o_t]
        oT = [oT[0], oT[1], oT[1]]
        PJ = {(1, "all"): qt_t[:, 0:1920], (0, "k"): qt_t[:, 1920:3840], (0, "q"): o_t[1][:, 0:Q_COLS],
              (2, "k"): re_t[:, 256:2176], (2, "q"): re_t[:, 256:2176]}
        PJ = {k: a.rearrange("p (b d) -> p b d", d=P) for k, a in PJ.items()}
        XR = sb("x_rows", D)
        XH = sb("x_norm", D)
        grow = [sb(f"ffn_gain_row{l}", D) for l in range(2)]
        V_t = sb("values", TILES * 256)
        V = V_t[:, :].rearrange("p (i d) -> p i d", d=256)
        kT_t = sb("keys_T", KV * T)
        kT = kT_t[:, :].rearrange("p (g k) -> p g k", k=T)
        kiT = sb("index_keys_T", T)
        qi_t = [None, sb("index_queries_T1", 2 * P), sb("index_queries_T2", 2 * P)]
        qiT = [None] + [a[:, :].rearrange("p (a n) -> p a n", n=P) for a in qi_t[1:]]
        WI_t = sb("index_weights", TILES * IDX_HEADS)
        WI = WI_t[:, :].rearrange("p (i h) -> p i h", i=TILES)
        BIAS = sb("bias", T)
        BIAS0 = sb("bias_T0", META)
        LATER = sb("later", T + 1)
        rope_t = sb("rope", TILES * 48)
        RO = rope_t[:, :].rearrange("p (i c) -> p i c", c=48)
        qg = sb("q_gain", P)
        kg = sb("k_gain", P)
        g_rows = XR[:, 512:640]
        gcol = sb("gain_columns", 40)
        sk_rows = XR[:, 0:512].rearrange("p (m d) -> p m d", d=P)
        skT_t = sb("subkeys_T", 4 * P)
        skT = skT_t[:, :].rearrange("p (m k) -> p m k", k=P)
        ident = sb("ident", P)
        zeros = sb("zeros", P)
        ones = sb("ones", 1)
        iota16 = sb("iota16", SEL)
        spread = XR[:, 640:880]
        SELW = sb("select_wide", 240)
        SG = sb("select_group", P)
        XS = sb("select_tokens", P)
        QG = sb("group_queries_T", 2 * P)
        S0 = sb("scores", 2 * P)
        S1 = sb("scores_left", 2 * P)
        top = sb("top_values", 32)
        top_i = sb("top_index", 32, U32)
        top_f = sb("top_index_f", 32)
        cand = sb("candidates", 256)
        cand2 = S1
        best = sb("best", SEL)
        pick = sb("pick", SEL, U32)
        pick_a = sb("pick_a", 2 * SEL, U32)
        pick_f = sb("pick_f", 2 * SEL)
        OH = sb("one_hot", 2 * 256)
        id_f = sb("id_f", 3 * SEL)
        IDU = [sb(f"ids_u{p}", SEL, U32) for p in range(2)]
        IDV = [sb(f"ids_v{p}", SEL, U32) for p in range(2)]
        nb0 = sb("minus_best", 1)
        GE = sb("gate_exp", SEL)
        GS = sb("gate_sum", 2)
        GA = [sb(f"gates{p}", SEL) for p in range(2)]
        DOT = sb("dots", SEL)
        GL = sb("gelu", SEL)
        AV = sb("activations", SEL)
        SSQ = sb("sum_squares", 11)
        MS = sb("mean_squares", 11)
        RT = sb("roots", 11)
        RS = sb("rstd", 11)
        nt_ = sb("newton", 1)
        hs = sb("head_sums", 40)
        red = sb("reductions", 24)
        m8 = sb("max8", 8)

        s_x = [sem(f"s_x{i}") for i in range(TILES)]
        s_small = sem("s_small")
        s_rope = sem("s_rope")
        s_win = [sem(f"s_win{c}") for c in range(KC)]
        s_wb = [sem(f"s_wb{k}") for k in range(WB)]
        s_wbu = sem("s_wbu")
        s_ev = sem("s_ev")
        s_grow = sem("s_grow")
        s_const = sem("s_const")
        s_constp = sem("s_constp")
        s_tr = sem("s_tr")
        s_setup = sem("s_setup")
        s_ssq = sem("s_ssq")
        s_ms = sem("s_ms")
        s_root = sem("s_root")
        s_rstd = sem("s_rstd")
        s_xh = sem("s_xh")
        s_xhT = sem("s_xhT")
        s_xT = sem("s_xT")
        s_proj = sem("s_proj")
        s_pj = sem("s_pj")
        s_pjd = sem("s_pjd")
        s_hms = sem("s_hms")
        s_hroot = sem("s_hroot")
        s_roped = sem("s_roped")
        s_qkT = sem("s_qkT")
        s_qk = sem("s_qk")
        s_qkd = sem("s_qkd")
        s_idx = sem("s_idx")
        s_relu = sem("s_relu")
        s_logit = sem("s_logit")
        s_zread = sem("s_zread")
        s_e1 = sem("s_e1")
        s_e2 = sem("s_e2")
        s_e3 = sem("s_e3")
        s_prob = sem("s_prob")
        s_probb = sem("s_probb")
        s_PTp = sem("s_PTp")
        s_PT = sem("s_PT")
        s_PTd = sem("s_PTd")
        s_pv = sem("s_pv")
        s_oT = sem("s_oT")
        s_wo = sem("s_wo")
        s_res = sem("s_res")
        s_ld = [sem(f"s_ld{k}") for k in range(16)]
        s_QG = sem("s_QG")
        s_XS = sem("s_XS")
        s_xr = sem("s_xr")
        s_xru = sem("s_xru")
        s_s = sem("s_s")
        s_S = sem("s_S")
        s_best = sem("s_best")
        s_gexp = sem("s_gexp")
        s_IDU = sem("s_IDU")
        s_IDV = sem("s_IDV")
        s_dots = sem("s_dots")
        s_gelu = sem("s_gelu")
        s_act = sem("s_act")
        s_DG = sem("s_DG")
        s_vused = sem("s_vused")
        s_fin = sem("s_fin")
        s_out = sem("s_out")
        s_dve = sem("s_dve")
        s_actc = sem("s_actc")
        s_carry = sem("s_carry")

        NORM = {("a", 1): 0, ("a", 0): 1, ("a", 2): 2, ("f0", 1): 3, ("f0", 0): 4, ("f0", 2): 5,
                ("b", 0): 6, ("b", 1): 7, ("f1", 1): 8, ("b", 2): 9, ("f1", 2): 10}
        XTC = [2, 4, 6, 8, 10, 12, 14, 18, 20, 24, 26]
        GAIN = {"a": 0, "kv": 1, "b": 2, "f0": 3, "f1": 4}
        PARTS = {(1, "all"): 1, (0, "k"): 2, (2, "k"): 3, (0, "q"): 4, (2, "q"): 5}
        WITH_Q = {(1, "all"): 1, (0, "q"): 2, (2, "q"): 3}
        WITH_K = {(1, "all"): 1, (0, "k"): 2, (2, "k"): 3}
        ATT = {(0, 1): 0, (0, 0): 1, (0, 2): 2, (1, 1): 3, (1, 2): 4}
        STEPS = {(0, 1): 0, (0, 2): 24, (1, 1): 48, (1, 2): 84}
        STREAM = ([("a_wo", m) for m in range(8)] + [("pq0", m) for m in range(16)]) * 2 + \
                 ([("kv", m) for m in range(4)] + [("b_wq", m) for m in range(8)] +
                  [("b_wo", m) for m in range(8)] + [("pq1", m) for m in range(16)]) * 2
        EV = [sum(k not in ("a_wo", "b_wo") for k, _ in STREAM[:b]) for b in range(len(STREAM) + 1)]
        WO_CHUNK = {(0, 1): 0, (0, 2): 2, (1, 1): 4, (1, 2): 6}
        PBANK = {(1, "all"): 0, (0, "k"): 6, (2, "k"): 6, (0, "q"): 4, (2, "q"): 6}
        KBANK = [4, 2, 6]
        def turn_bank(l, i, g, j):
            return 2 * g + j if (l, i) == (0, 1) else (0, 4, 5)[j]

        def pv_bank(l, i, g):
            return 4 + g if (l, i) == (0, 1) else 3

        def logit_banks(l, i, g):
            n, keys = NT[i], KEYS[i]
            if (l, i) == (0, 1):
                return bank[:n, 2 * g:2 * g + 2, :].rearrange("p b (t k) -> p (b t) k", k=256)[:, :, :keys]
            return bank[:n, 0:4, :keys]

        def weights_at(l, i, g):
            return XH[:, :].rearrange("p (j m) -> p j m", m=512) if (l, i, g) == (0, 1, 1) else PT

        def logits_at(l, i, g):
            return R4 if (l, i, g) == (0, 1, 1) else L

        PTD = {(0, 1): 0, (0, 2): 2, (1, 1): 4, (1, 2): 6}
        LOOPED = (1, 2)
        FIN = {(0, 1): 1, (0, 0): 2, (0, 2): 3, (1, 1): 4, (1, 2): 5}

        HEAD_RANGE = {"all": (0, 10), "q": (0, 8), "k": (8, 10)}

        def first_block(l, i, kind):
            at = {"wo": 0, "pq": 8} if l == 0 else {"kv": 0, "bq": 4, "wo": 12, "pq": 20}
            return STEPS[l, i] + at[kind]

        def group_no(l, i, j):
            return {(0, 1): 0, (0, 0): 8, (0, 2): 9, (1, 1): 17, (1, 2): 25}[l, i] + j

        def group_at(i, j):
            return {1: 0, 0: 8, 2: 9}[i] + j

        ROUTE = 7
        def half_work(l, i, g, slots=(0, 0, 2, 4, 6, 7)):
            return [(k, name, l, i, g) for k, name in zip(slots, ("logits", "soft_a", "soft_b", "turn", "turned", "pv"))]

        def norm_work(k, kind, i):
            return [(k, "norm", kind, i), (k + 1, "xhT", kind, i), (k + 2, "xT", kind, i)]

        def blocks_work(name, what, blocks, slots):
            return [(k, name, *what, m) for m, k in zip(blocks, slots, strict=True)]

        def attention_b(i):
            wo = [("wo", (1, i)), ("pq", (1, i))]
            return {1: ((norm_work(0, "b", 0) if i == 1 else []) + norm_work(2, "b", i) +
                        blocks_work("kv", (i,), range(0, 4), (6, 9, 11, 13)) + blocks_work("bq", (i,), range(0, 1), (15,))),
                    2: blocks_work("bq", (i,), range(1, 8), (1, 3, 5, 7, 10, 12, 14)),
                    3: half_work(1, i, 0),
                    4: half_work(1, i, 1) + blocks_work(*wo[0], range(0, 4), (8, 10, 12, 14)) +
                       [(15, "res", 1, i, 0)],
                    5: (blocks_work(*wo[0], range(4, 8), (0, 2, 4, 6)) + [(7, "res", 1, i, 1)] +
                        norm_work(8, "f1", i) + blocks_work(*wo[1], range(0, 3), (11, 13, 15))),
                    6: blocks_work(*wo[1], range(3, 11), (0, 2, 4, 6, 9, 11, 13, 15)),
                    7: blocks_work(*wo[1], range(11, 16), (0, 1, 3, 5, 6))}

        wo_a, pq_a = ("wo", (0, 2)), ("pq", (0, 2))
        work = {(0, 1, 0): [(0, "project", 0, "q"), (ROUTE + 1, "project", 2, "q")],
                (0, 1, 1): [(1, "qk", 0, "q"), (2, "qkT", 0, "q"), (3, "qk_out", 0, "q"),
                            (4, "qk", 2, "q"), (6, "qkT", 2, "q"), (6, "qk_out", 2, "q")],
                (0, 1, 2): half_work(0, 0, 0, (0, 0, 0, 1, 1, 2)) + half_work(0, 0, 1, (3, 3, 3, 4, 4, 5)),
                (0, 1, 3): half_work(0, 2, 0),
                (0, 1, 4): half_work(0, 2, 1) + blocks_work(*wo_a, range(0, 4), (8, 10, 12, 14)),
                (0, 1, 5): ([(0, "res", 0, 2, 0)] + blocks_work(*wo_a, range(4, 8), (1, 3, 5, 6)) + [(7, "res", 0, 2, 1)] +
                            norm_work(8, "f0", 0) + norm_work(10, "f0", 2) + blocks_work(*pq_a, range(0, 2), (13, 15))),
                (0, 1, 6): blocks_work(*pq_a, range(2, 10), (0, 2, 4, 6, 9, 11, 13, 15)),
                (0, 1, 7): blocks_work(*pq_a, range(10, 16), (0, 1, 3, 4, 5, 6))}
        for l, i, nxt in ((0, 2, 1), (1, 1, 2)):
            for j, steps in attention_b(nxt).items():
                work[l, i, j] = steps
        IN_ROW_BANKS = ("qkT", "logits")
        ORDER = [(0, 1), (0, 0), (0, 2), (1, 1), (1, 2)]
        GROUPS = [(l, i, j) for l, i in ORDER for j in range(8 if i else 1)]
        RING = 8

        def before(l, i, j):
            if not number(j):
                return l, i, j - 1
            n = group_no(l, i, j)
            return GROUPS[n - 1] if n else None

        def after(l, i, j):
            if not number(j):
                return l, i, j + 1
            n = group_no(l, i, j)
            return GROUPS[n + 1] if n + 1 < len(GROUPS) else None

        def number(n):
            return isinstance(n, int)

        def ends(l, i, j):
            return number(j) and j == (7 if i else 0)

        def walk(eng, step, chain=None, per=0):
            for l, i in ORDER:
                if (l, i) != LOOPED:
                    for j in range(8 if i else 1):
                        step(l, i, j, group_no(l, i, j) % 2)
                    continue
                step(l, i, 0, group_no(l, i, 0) % 2)
                start = chain.n if chain else 0
                with eng.Fori(0, 3) as t:
                    if chain:
                        chain.off = t * (2 * per)
                    for q in (1, 2):
                        step(l, i, 2 * t + q, (group_no(l, i, 0) + q) % 2)
                if chain:
                    assert chain.n - start == 2 * per, (chain.n - start, per)
                    chain.n, chain.off = start + 6 * per, 0
                step(l, i, 7, group_no(l, i, 7) % 2)

        def gaps(steps, l, i, j, slot):
            if number(j):
                for k, name, *what in work.get((l, i, j), ()):
                    if k == slot and name in steps:
                        steps[name](*what)

        block = ctx.enter_context(nc.Block())

        @block.sync
        def _(sp):
            sp.dma_start(hx[:, 1, :], x[0, 0:P, :]).then_inc(s_x[1], 16)
            sp.dma_start(hx[:META, 0, :], meta).then_inc(s_x[0], 16)
            for n, g in enumerate((a_norm[0], kv_norm, b_norm[0], ffn_norm[0], ffn_norm[1])):
                sp.dma_start(g_rows[8 * n:8 * n + 8, :], g.rearrange("(c p) -> c p", p=P)).then_inc(s_small, 16)
            sp.dma_start(sk_rows, peer_subkeys.rearrange("l c k d -> k (l c) d")).then_inc(s_small, 16)
            w_rows = a_w_in[0].rearrange("(c p) n -> p c n", p=P)
            for c in range(KC):
                sp.dma_start(w_q[:, c, :], w_rows[:, c, 0:Q_COLS]).then_inc(s_win[c], 16)
                sp.dma_start(w_r[:, c, :], w_rows[:, c, Q_COLS:A_COLS]).then_inc(s_win[c], 16)
                if c == 0:
                    sp.dma_start(hx[:, 2, :], x[0, P:2 * P, :]).then_inc(s_x[2], 16)
                if c == 1:
                    sp.dma_start(RO[:META, 0, :], rope[0:META, :]).then_inc(s_rope, 16)
                    sp.dma_start(RO[:, 1:3, :], rope[META:T, :].rearrange("(i p) c -> p i c", p=P)).then_inc(s_rope, 16)
                    sp.dma_start(qg[:, :], a_q_norm.broadcast_to([P, P])).then_inc(s_rope, 16)
                    sp.dma_start(kg[:, :], a_k_norm.broadcast_to([P, P])).then_inc(s_rope, 16)
            for l in range(2):
                sp.dma_start(grow[l][:, :], ffn_norm[l:l + 1].broadcast_to([P, D])).then_inc(s_grow, 16)
            rows = {"a_wo": a_w_o[0], "b_wo": b_w_o[0], "pq0": peer_w_q[0], "pq1": peer_w_q[1], "kv": kv_w,
                    "b_wq": b_w_q[0]}
            rows = {k: w.rearrange("(c p) n -> p c n", p=P) for k, w in rows.items()}
            stored = 0
            for b, (kind, m) in enumerate(STREAM):
                if b >= WB:
                    sp.wait_ge(s_wbu, b - WB + 1)
                sp.dma_start(wb[:, b % WB, :, :], rows[kind][:, :, P * m:P * m + P]).then_inc(s_wb[b % WB], 16)
            for i in (1, 2):
                sp.wait_ge(s_fin, FIN[1, i])
                sp.dma_start(out[0, (i - 1) * P:i * P, :], hx[:, i, :]).then_inc(s_out, 16)
            sp.wait_ge(s_out, 32)

        @block.gpsimd
        def _(pool):
            pool.memset(ident[:, :], 0.0)
            pool.memset(spread, 0.0)
            pool.memset(zeros[:, :], 0.0)
            pool.memset(ones[:, :], 1.0)
            pool.memset(l_t[:, :], 0.0)
            pool.memset(BIAS0[:, :], 0.0)
            pool.memset(LATER[:, :], -MASKED)
            pool.iota(iota16[:, :], pattern=[[1, SEL]], base=0, channel_multiplier=0,
                      allow_small_or_imprecise_dtypes=True).then_inc(s_constp, 1)
            pool.wait_ge(s_constp, 1)
            pool.affine_select(out=ident[:, :], in_=ident[:, :], compare_op=ALU.not_equal, fill=1.0, base=0,
                               pattern=[[-1, P]], channel_multiplier=1).then_inc(s_constp, 1)
            pool.wait_ge(s_constp, 2)
            pool.tensor_copy(XS[:GT, :].rearrange("p (h t) -> p h t", t=GT),
                             ident[:GT, :GT].unsqueeze(1).broadcast_to([GT, HEADS, GT]))
            pool.affine_select(out=spread[:GT, :], in_=spread[:GT, :], compare_op=ALU.not_equal, fill=1.0,
                               base=112, pattern=[[-1, 240]], channel_multiplier=1)
            pool.affine_select(out=LATER[:, :], in_=LATER[:, :], compare_op=ALU.is_ge, fill=MASKED,
                               base=P + META, pattern=[[-1, T + 1]], channel_multiplier=1)
            pool.affine_select(out=BIAS0[:META, :], in_=BIAS0[:META, :], compare_op=ALU.is_ge,
                               fill=NEG, base=0, pattern=[[-1, META]], channel_multiplier=1).then_inc(s_const, 1)

            def gather(table, ids, k, slot):
                pool.indirect_dma_start(
                    out=ring[:, slot, :], out_offset=None, in_=table,
                    in_offset=bass.IndirectOffsetOnAxis(ap=ids[:, k:k + 1], axis=0)).then_inc(s_ld[slot], 16)

            def carry(n):
                if not number(n):
                    pool.sem_inc(s_carry, 1)

            def u_rows_of(n, par, k):
                if k == 0:
                    pool.wait_ge(s_IDU, n + 1)
                    carry(n)
                    if number(n) and n == 0:
                        pool.wait_ge(s_proj, PARTS[2, "k"])
                if not (number(n) and 16 * n + k < RING):
                    pool.wait_ge(s_dots, 16 * n + k + 1 - RING)
                    carry(n)
                gather(u_rows, IDU[par], k, k % RING)

            def v_rows_of(n, par, k):
                if k == 0:
                    pool.wait_ge(s_IDV, n + 1)
                    carry(n)
                    if number(n) and n == 0:
                        pool.wait_ge(s_proj, PARTS[2, "q"])
                if not (number(n) and 16 * n + k < RING):
                    pool.wait_ge(s_vused, 16 * n + k + 1 - RING)
                    carry(n)
                gather(v_rows, IDV[par], k, RING + k % RING)

            def step(l, i, j, par):
                n = group_no(l, i, j)
                for k in range(16):
                    u_rows_of(n, par, k)
                    if not (number(n) and n == 0):
                        v_rows_of(n - 1, 1 - par, k)

            walk(pool, step)
            for k in range(16):
                v_rows_of(len(GROUPS) - 1, (len(GROUPS) - 1) % 2, k)

        @block.scalar
        def _(act):
            c = Chain(act, s_actc)
            A = act.activation

            def norm(kind, i):
                k, n = NORM[kind, i], NT[i]
                if k:
                    act.wait_ge(s_xhT, 2 * k)
                if kind == "a":
                    act.wait_ge(s_x[i], 16)
                elif kind == "b":
                    act.wait_ge(s_fin, FIN[0, i])
                elif i:
                    act.wait_ge(s_res, WO_CHUNK[0 if kind == "f0" else 1, i] + 2)
                A(XH[:n, :], hx[:n, i, :], ACT.Square, accum_out=SSQ[:n, k:k + 1]).then_inc(s_ssq, 1)
                act.wait_ge(s_ms, k + 1)
                A(RT[:n, k:k + 1], MS[:n, k:k + 1], ACT.Sqrt).then_inc(s_root, 1)
                act.wait_ge(s_rstd, k + 1)
                A(XH[:n, :], hx[:n, i, :], ACT.Copy, scale=RS[:n, k:k + 1]).then_inc(s_xh, 1)

            def project(i, part):
                n, b, pj = NT[i], PBANK[i, part], PJ[i, part]
                act.wait_ge(s_proj, PARTS[i, part])
                if part != "k":
                    ins = A(pj[:n, 0:8, :], bank[:n, b:b + 2, :].rearrange("p b (h d) -> p (b h) d", d=P), ACT.Copy)
                    b += 2
                if part != "q":
                    if i == 0:
                        ins = A(pj[:n, 14, 0:64], bank[:n, b + 1, 0:64], ACT.Copy)
                    else:
                        A(pj[:n, 12:15, :].rearrange("p b d -> p (b d)")[:, 0:320], bank[:n, b + 1, 0:320], ACT.Copy)
                        ins = A(WI[:n, i, :], bank[:n, b + 1, 320:324], ACT.Copy)
                ins.then_inc(s_pj, 1)

            def qk(i, part):
                n, h0, h1 = NT[i], *HEAD_RANGE[part]
                act.wait_ge(s_hms, PARTS[i, part])
                A(hs[:n, 20 + h0:20 + h1], hs[:n, h0:h1], ACT.Sqrt).then_inc(s_hroot, 1)

            def qk_out(i, part):
                n = NT[i]
                act.wait_ge(s_qkT, PARTS[i, part])
                src = bank[:, 0:2, :].rearrange("p b (h n) -> p (b h) n", n=n) if n == P else \
                    bank[:, 0, :8 * n].rearrange("p (h n) -> p h n", n=n)
                A(qT[i][:, :, :], src, ACT.Copy).then_inc(s_qk, 1)

            def select(i):
                n = NT[i]
                act.wait_ge(s_idx, i)
                A(R4[:n, :, :KEYS[i]], bank[:n, 0:4, :KEYS[i]], ACT.Relu, scale=IDX_SCALE).then_inc(s_relu, 1)

            def soft(l, i, g):
                n, keys, t = NT[i], KEYS[i], ATT[l, i]
                u = 2 * t + g
                act.wait_ge(s_e1, u + 1)
                if l == 0:
                    z = logits_at(l, i, g)[:n, :, :keys]
                    A(z, z, ACT.Exp).then_inc(s_e2, 1)
                else:
                    c.do(A(E4[:n, :, :keys], E4[:n, :, :keys], ACT.Exp, scale=-1.0))
                    A(E4[:n, :, :keys], E4[:n, :, :keys], ACT.Ln, bias=1.0).then_inc(s_e2, 1)
                    act.wait_ge(s_e3, u - 6 + 1)
                    A(L[:n, :, :keys], L[:n, :, :keys], ACT.Exp).then_inc(s_probb, 1)

            def turned(l, i, g):
                n, u = NT[i], 2 * ATT[l, i] + g
                act.wait_ge(s_PTp, u + 1)
                A(weights_at(l, i, g)[:n, i, :GROUP * n], bank[:n, turn_bank(l, i, g, i), :GROUP * n], ACT.Copy).then_inc(s_PT, 1)

            def pv(l, i, g):
                n, u = NT[i], 2 * ATT[l, i] + g
                act.wait_ge(s_pv, u + 1)
                A(oT[i][:, GROUP * g:GROUP * (g + 1), :],
                  bank[:, pv_bank(l, i, g), :GROUP * n].rearrange("p (h n) -> p h n", n=n), ACT.Copy).then_inc(s_oT, 1)

            def copied(b, dst, src):
                act.wait_ge(s_wbu, b + 1)
                return A(dst, src, ACT.Copy)

            def pq(l, i, m):
                b = first_block(l, i, "pq") + m
                with_0 = l == 0 and i == 2
                g0, g1 = (8 if with_0 else group_at(i, 0)), group_at(i, 0) + 8
                w = GT * (g1 - g0)
                copied(b, QTw[:, m % 2, g0:g1, m // 2, :],
                       bank[:, 3 + EV[b] % 3, :w].rearrange("p (g t) -> p g t", t=GT)).then_inc(s_ev, 1)

            def kv(i, m):
                b = first_block(1, i, "kv") + m
                k = 3 + EV[b] % 3
                if m < 2:
                    a, w = (0, META + P) if i == 1 else (META + P, P)
                    copied(b, kT[:, m, a:a + w], bank[:, k, :w]).then_inc(s_ev, 1)
                else:
                    d = slice(P * (m - 2), P * (m - 1))
                    if i == 1:
                        copied(b, V[:META, 0, d], bank[:META, k, P:2 * P])
                    copied(b, V[:, i, d], bank[:, k, :P]).then_inc(s_ev, 1)

            def bq(i, m):
                b = first_block(1, i, "bq") + m
                copied(b, qT[i][:, m, :], bank[:, 3 + EV[b] % 3, :P]).then_inc(s_ev, 1)

            gap = {"norm": norm, "project": project, "qk": qk, "qk_out": qk_out, "soft_a": soft, "turned": turned,
                   "pv": pv, "pq": pq, "kv": kv, "bq": bq}

            act.wait_ge(s_const, 1)
            for i in (1, 0, 2):
                norm("a", i)
            project(1, "all")
            qk(1, "all")
            project(0, "k")
            qk(0, "k")
            qk_out(1, "all")
            select(1)
            for g in range(2):
                soft(0, 1, g)
            project(2, "k")
            for g in range(2):
                turned(0, 1, g)
            for g in range(2):
                pv(0, 1, g)
            qk(2, "k")
            norm("f0", 1)
            select(2)
            for m in range(16):
                pq(0, 1, m)
            act.wait_ge(s_ev, 16)

            def route(l, i, j):
                n = group_no(l, i, j)
                first = number(n) and n == 0

                def carry():
                    if not number(n):
                        act.sem_inc(s_carry, 1)

                r = NORM[("f0", "f1")[l], i]
                nt = NT[i]
                g = group_at(i, j)
                if not first:
                    act.wait_ge(s_s, n)
                    carry()
                if number(j) and j == 0:
                    act.wait_ge(s_ev, EV[first_block(l, i or 2, "pq") + 16])
                A(QG[:, :].rearrange("p (c m) -> p c m", c=2), QT[:, :, bass.ds(g, 1), :].rearrange("p c o m -> p c (o m)"),
                  ACT.Copy).then_inc(s_QG, 1)
                if not first:
                    act.wait_ge(s_xr, n)
                    carry()
                A(XS[:nt, :].rearrange("p (h t) -> p h t", t=GT),
                  ident[:nt, bass.ds(16 * j, 16)].unsqueeze(1).broadcast_to([nt, HEADS, GT]),
                  ACT.Copy, scale=RS[:nt, r:r + 1]).then_inc(s_XS, 1)
                if not first:
                    act.wait_ge(s_IDU, n)
                act.wait_ge(s_s, n + 1)
                A(S0[:, :], bank[:, 2, 0:2 * P], ACT.Copy).then_inc(s_S, 1)
                act.wait_ge(s_best, n + 1)
                A(GE[:, :], best[:, :], ACT.Exp, bias=nb0[:, :], accum_out=GS[:, 0:1]).then_inc(s_gexp, 1)

            def step(l, i, j, par):
                n = group_no(l, i, j)
                first = number(n) and n == 0

                def carry():
                    if not number(n):
                        act.sem_inc(s_carry, 1)

                for k in range(16):
                    gaps(gap, l, i, j, k)
                    if k == ROUTE and after(l, i, j):
                        route(*after(l, i, j))
                act.wait_ge(s_dots, 16 * n + 16)
                A(GL[:, :], DOT[:, :], ACT.Gelu).then_inc(s_gelu, 1)
                if not first:
                    act.wait_ge(s_DG, 16 * n)
                    carry()
                c.do(A(SG[:, :], SELW[:, bass.ds(112 - 16 * j, P)], ACT.Copy))
                act.wait_ge(s_act, n + 1)
                for k in range(16):
                    if not first and k % 4 == 0:
                        act.wait_ge(s_vused, 16 * (n - 1) + k + 4)
                    A(DG[:, k, :], SG[:, :], ACT.Copy, scale=AV[:, k:k + 1]).then_inc(s_DG, 1)

            route(*GROUPS[0])
            walk(act, step, c, 1)

        @block.vector
        def _(dve):
            c = Chain(dve, s_dve)
            tt, ts, stt = dve.tensor_tensor, dve.tensor_scalar, dve.scalar_tensor_tensor

            dve.wait_ge(s_tr, 1)
            dve.tensor_copy(gcol[:, :], bank[:, 0, 0:40])
            dve.tensor_copy(skT[:, :, :], bank[:, 1, :].rearrange("p (m k) -> p m k", k=P))
            dve.tensor_copy(SELW[:, :], bank[:, 2, 0:240]).then_inc(s_setup, 1)
            dve.wait_ge(s_setup, 1)

            def inverse_root(dst, ms, root, tmp):
                c.do(dve.reciprocal(dst, root))
                c.do(tt(tmp, ms, dst, ALU.mult))
                c.do(tt(tmp, tmp, dst, ALU.mult))
                c.do(ts(tmp, tmp, -0.5, 1.5, ALU.mult, ALU.add))
                return tt(dst, dst, tmp, ALU.mult)

            def norm(kind, i):
                k, n = NORM[kind, i], NT[i]
                dve.wait_ge(s_ssq, k + 1)
                ts(MS[:n, k:k + 1], SSQ[:n, k:k + 1], 1.0 / D, EPS, ALU.mult, ALU.add).then_inc(s_ms, 1)
                dve.wait_ge(s_root, k + 1)
                inverse_root(RS[:n, k:k + 1], MS[:n, k:k + 1], RT[:n, k:k + 1], nt_[:n, 0:1]).then_inc(s_rstd, 1)

            def xt(kind, i):
                k, n = NORM[kind, i], NT[i]
                o = META if i else 0
                if kind == "a":
                    outs = [("a", xT if i == 1 else xT2)]
                elif kind == "b":
                    outs = [("kv", xT2)] + ([("b", xT)] if i else [])
                else:
                    outs = [(kind, xT)]
                for hf in range(2):
                    dve.wait_ge(s_xhT, 2 * k + hf + 1)
                    src = bank[:, 4 + hf, :4 * n].rearrange("p (c n) -> p c n", n=n)
                    for gain, dst in outs:
                        a = GAIN[gain] * 8 + 4 * hf
                        tt(dst[:, 4 * hf:4 * hf + 4, o:o + n], src,
                           gcol[:, a:a + 4].unsqueeze(2).broadcast_to([P, 4, n]), ALU.mult).then_inc(s_xT, 1)

            def rotate(view, i, hd, at, heads):
                n = NT[i]
                cos = RO[:n, i, at:at + hd].unsqueeze(1).broadcast_to([n, heads, hd])
                sin = RO[:n, i, at + hd:at + 2 * hd].unsqueeze(1).broadcast_to([n, heads, hd])
                a, b = view[:, :, 0:hd], view[:, :, hd:2 * hd]
                w = heads * hd
                t = [TMP[:n, m * w:(m + 1) * w].rearrange("p (h d) -> p h d", d=hd) for m in range(4)]
                tt(t[0], a, cos, ALU.mult)
                tt(t[1], b, sin, ALU.mult)
                tt(t[2], b, cos, ALU.mult)
                c.do(tt(t[3], a, sin, ALU.mult))
                tt(a, t[0], t[1], ALU.subtract)
                return tt(b, t[2], t[3], ALU.add)

            def project(i, part):
                n, b = NT[i], PBANK[i, part] + (2 if part == "all" else 0)
                dve.wait_ge(s_proj, PARTS[i, part])
                dve.tensor_copy(PJ[i, part][:n, 8:10, :], bank[:n, b, 0:256].rearrange("p (b d) -> p b d", d=P))
                dve.tensor_copy(V[:n, i, :], bank[:n, b, 256:512]).then_inc(s_pjd, 1)

            def qk(i, part):
                n, p, pj = NT[i], PARTS[i, part], PJ[i, part]
                h0, h1 = HEAD_RANGE[part]
                heads = h1 - h0
                dve.wait_ge(s_pj, p)
                if part != "q":
                    dve.wait_ge(s_pjd, WITH_K[i, part])
                qk = pj[:n, h0:h1, :]
                ms, rs, rt, tmp = (hs[:n, 10 * m + h0:10 * m + h1] for m in range(4))
                if p > 1:
                    dve.wait_ge(s_roped, p - 1)
                if (i, part) == (2, "k"):
                    dve.wait_ge(s_pv, 2)
                sq = TMP[:n, :heads * P].rearrange("p (h d) -> p h d", d=P)
                c.do(tt(sq, qk, qk, ALU.mult))
                c.do(dve.reduce_sum(ms, sq, AX.X))
                ts(ms, ms, 1.0 / P, EPS, ALU.mult, ALU.add).then_inc(s_hms, 1)
                if part != "q":
                    index = pj[:n, 12:15, :].rearrange("p b (t d) -> p (b t) d", d=64)
                    a = 0 if i else 4
                    c.do(rotate(index[:, a:5, :], i, 8, 32, 5 - a))
                    dve.tensor_copy(pj[:n, 14, 64:128], pj[:n, 14, 0:64])
                dve.wait_ge(s_hroot, p)
                c.do(inverse_root(rs, ms, rt, tmp))
                c.do(tt(qk, qk, rs.unsqueeze(2).broadcast_to([n, heads, P]), ALU.mult))
                if part != "k":
                    ins = tt(pj[:n, 0:8, :], pj[:n, 0:8, :], qg[:n, :].unsqueeze(1).broadcast_to([n, 8, P]), ALU.mult)
                if part != "q":
                    ins = tt(pj[:n, 8:10, :], pj[:n, 8:10, :], kg[:n, :].unsqueeze(1).broadcast_to([n, 2, P]), ALU.mult)
                c.do(ins)
                rotate(qk, i, 16, 0, heads).then_inc(s_roped, 1)

            def k_out(i, part):
                n, b = NT[i], KBANK[i]
                dve.wait_ge(s_qkT, PARTS[i, part])
                if n == P:
                    dve.tensor_copy(kT[:, :, OFF[i]:OFF[i] + n], bank[:, b, 0:256].rearrange("p (h n) -> p h n", n=n))
                    dve.tensor_copy(qiT[i][:, :, :], bank[:, b, 256:512].rearrange("p (h n) -> p h n", n=n))
                    c.do(dve.tensor_copy(kiT[:, OFF[i]:OFF[i] + n], bank[:, b + 1, 0:n]))
                else:
                    src = bank[:, b, :3 * n].rearrange("p (h n) -> p h n", n=n)
                    dve.tensor_copy(kT[:, :, :n], src[:, 0:2, :])
                    c.do(dve.tensor_copy(kiT[:, :n], src[:, 2, :]))
                dve.sem_inc(s_qkd, 1)

            def later(i, strict):
                a = P + META - OFF[i] + strict
                return LATER[:NT[i], a:a + KEYS[i]]

            def select(i):
                n, keys = NT[i], KEYS[i]
                dve.wait_ge(s_relu, i)
                c.do(ts(SC[:n, :keys], R4[:n, 0, :keys], WI[:n, i, 0:1], None, ALU.mult))
                for h in range(1, IDX_HEADS):
                    c.do(stt(SC[:n, :keys], R4[:n, h, :keys], WI[:n, i, h:h + 1], SC[:n, :keys], ALU.mult, ALU.add))
                c.do(tt(SC[:n, :keys], SC[:n, :keys], later(i, 0), ALU.min))
                for r in range(TOPK // 8):
                    src, dst = (SC, WK) if r % 2 == 0 else (WK, SC)
                    c.do(dve.max(m8[:n, :], src[:n, :keys]))
                    c.do(dve.match_replace(dst[:n, :keys], m8[:n, :], src[:n, :keys], TAKEN))
                c.do(ts(BIAS[:n, :keys], dst[:n, :keys], TAKEN_BELOW, NEG, ALU.is_gt, ALU.mult))
                c.do(tt(BIAS[:n, :keys], BIAS[:n, :keys], later(i, 0), ALU.min))

            def turned(l, i, g):
                n, u = NT[i], 2 * ATT[l, i] + g
                if i:
                    dve.wait_ge(s_PTp, u + 1)
                    for j in range(i):
                        kn = NT[j]
                        ins = dve.tensor_copy(weights_at(l, i, g)[:kn, j, :GROUP * n], bank[:kn, turn_bank(l, i, g, j), :GROUP * n])
                    ins.then_inc(s_PTd, 1)

            def soft_a(l, i, g):
                n, keys = NT[i], KEYS[i]
                u, r = 2 * ATT[l, i] + g, 12 * g
                z = logits_at(l, i, g)[:n, :, :keys]
                dve.wait_ge(s_logit, u + 1)
                if l == 0:
                    bias = BIAS[:n, :keys] if i else BIAS0[:n, :]
                    stt(z, logit_banks(l, i, g), SCALE, bias.unsqueeze(1).broadcast_to([n, GROUP, keys]),
                        ALU.mult, ALU.add).then_inc(s_zread, 1)
                    dve.wait_ge(s_zread, u + 1)
                    c.do(dve.reduce_max(red[:n, r:r + 4], z, AX.X))
                    tt(z, z, red[:n, r:r + 4].unsqueeze(2).broadcast_to([n, GROUP, keys]), ALU.subtract).then_inc(s_e1, 1)
                else:
                    ts(z, logit_banks(l, i, g), SCALE, None, ALU.mult).then_inc(s_zread, 1)
                    dve.wait_ge(s_zread, u + 1)
                    stt(E4[:n, :, :keys], z, -1.0, z, ALU.mult, ALU.max).then_inc(s_e1, 1)

            def soft_b(l, i, g):
                n, keys = NT[i], KEYS[i]
                u, r = 2 * ATT[l, i] + g, 12 * g
                z = logits_at(l, i, g)[:n, :, :keys]
                dve.wait_ge(s_e2, u + 1)
                if l == 0:
                    c.do(dve.reduce_sum(red[:n, r + 4:r + 8], z, AX.X))
                    c.do(dve.reciprocal(red[:n, r + 8:r + 12], red[:n, r + 4:r + 8]))
                    tt(z, z, red[:n, r + 8:r + 12].unsqueeze(2).broadcast_to([n, GROUP, keys]), ALU.mult).then_inc(s_prob, 1)
                    return
                e, cs = E4[:n, :, :keys], C4[:n, :, :keys]
                c.do(stt(e, z, 0.0, e, ALU.max, ALU.add))
                mask = later(i, 1).unsqueeze(1).broadcast_to([n, GROUP, keys])
                c.do(stt(e, mask, 0.0, e, ALU.is_gt, ALU.mult))
                for h in range(GROUP):
                    ins = dve.tensor_tensor_scan(C4[:n, h, 0:keys][:, ::-1], ones[:n, :].broadcast_to([n, keys]),
                                                 E4[:n, h, 0:keys][:, ::-1], 0.0, ALU.mult, ALU.add)
                c.do(ins)
                c.do(tt(z, z, cs, ALU.subtract))
                tt(z, z, mask, ALU.min).then_inc(s_e3, 1)

            def res(l, i, m):
                q = WO_CHUNK[l, i] + m
                dve.wait_ge(s_wo, q + 1)
                d = slice(512 * m, 512 * m + 512)
                if (l, i) == (0, 2):
                    tt(hx[:META, 0, d], hx[:META, 0, d], bank[:META, 4, :], ALU.add)
                tt(hx[:, i, d], hx[:, i, d], bank[:, 3 + 2 * m, :], ALU.add).then_inc(s_res, 1)

            gap = {"norm": norm, "xT": xt, "qk": qk, "soft_a": soft_a, "soft_b": soft_b, "turned": turned, "res": res}

            for i in (1, 0, 2):
                norm("a", i)
                xt("a", i)
            dve.wait_ge(s_rope, 64)
            project(1, "all")
            qk(1, "all")
            project(0, "k")
            qk(0, "k")
            k_out(1, "all")
            k_out(0, "k")
            select(1)
            for g in range(2):
                soft_a(0, 1, g)
            for g in range(2):
                soft_b(0, 1, g)
            project(2, "k")
            for g in range(2):
                turned(0, 1, g)
            qk(2, "k")
            res(0, 1, 0)
            k_out(2, "k")
            res(0, 1, 1)
            norm("f0", 1)
            xt("f0", 1)
            select(2)
            dve.wait_ge(s_grow, 32)

            def route(l, i, j, par):
                n = group_no(l, i, j)

                def carry():
                    if not number(n):
                        dve.sem_inc(s_carry, 1)

                dve.wait_ge(s_S, n + 1)
                carry()
                for h in range(2):
                    s = slice(P * h, P * h + P)
                    ins = dve.max(top[:, 16 * h:16 * h + 8], S0[:, s])
                c.do(ins)
                carry()
                for h in range(2):
                    s, t = slice(P * h, P * h + P), slice(16 * h, 16 * h + 8)
                    dve.max_index(top_i[:, t], top[:, t], S0[:, s])
                    ins = dve.match_replace(S1[:, s], top[:, t], S0[:, s], TAKEN)
                c.do(ins)
                carry()
                for h in range(2):
                    s = slice(P * h, P * h + P)
                    ins = dve.max(top[:, 16 * h + 8:16 * h + 16], S1[:, s])
                c.do(ins)
                carry()
                for h in range(2):
                    s, t = slice(P * h, P * h + P), slice(16 * h + 8, 16 * h + 16)
                    dve.max_index(top_i[:, t], top[:, t], S1[:, s])
                a = top[:, 0:16].unsqueeze(2).broadcast_to([P, 16, 16])
                b = top[:, 16:32].unsqueeze(1).broadcast_to([P, 16, 16])
                c.do(tt(cand[:, :].rearrange("p (a b) -> p a b", b=16), a, b, ALU.add))
                carry()
                c.do(dve.max(best[:, 0:8], cand[:, :]))
                carry()
                dve.max_index(pick[:, 0:8], best[:, 0:8], cand[:, :])
                c.do(dve.match_replace(cand2[:, :], best[:, 0:8], cand[:, :], TAKEN))
                carry()
                c.do(dve.max(best[:, 8:16], cand2[:, :]))
                carry()
                dve.max_index(pick[:, 8:16], best[:, 8:16], cand2[:, :])
                ts(nb0[:, :], best[:, 0:1], -1.0, None, ALU.mult).then_inc(s_best, 1)
                dve.wait_ge(s_best, n + 1)
                ts(pick_a[:, 0:16], pick[:, :], 4, None, ALU.logical_shift_right)
                ts(pick_a[:, 16:32], pick[:, :], 15, None, ALU.bitwise_and)
                c.do(dve.tensor_copy(top_f[:, :], top_i[:, :]))
                c.do(dve.tensor_copy(pick_f[:, :], pick_a[:, :]))
                oh = OH[:, :].rearrange("p (k a) -> p k a", a=16)
                c.do(tt(oh, pick_f[:, :].unsqueeze(2).broadcast_to([P, 32, 16]),
                        iota16[:, :].unsqueeze(1).broadcast_to([P, 32, 16]), ALU.is_equal))
                for h in range(2):
                    ins = tt(oh[:, 16 * h:16 * h + 16, :], oh[:, 16 * h:16 * h + 16, :],
                             top_f[:, 16 * h:16 * h + 16].unsqueeze(1).broadcast_to([P, 16, 16]), ALU.mult)
                c.do(ins)
                c.do(dve.reduce_sum(id_f[:, 0:32], oh, AX.X))
                c.do(stt(id_f[:, 32:48], id_f[:, 0:16], float(NKEYS), id_f[:, 16:32], ALU.mult, ALU.add))
                ts(IDU[par][:, :], id_f[:, 32:48], float(EXPERTS * l), None, ALU.add).then_inc(s_IDU, 1)
                dve.wait_ge(s_gexp, n + 1)
                c.do(dve.reciprocal(GS[:, 1:2], GS[:, 0:1]))
                c.do(ts(GA[par][:, :], GE[:, :], GS[:, 1:2], None, ALU.mult))

            def step(l, i, j, par):
                n = group_no(l, i, j)
                first = number(n) and n == 0
                dve.wait_ge(s_xr, n + 1)
                tt(XR[:, :], bank[:, 0:2, :].rearrange("p b n -> p (b n)"), grow[l][:, :], ALU.mult).then_inc(s_xru, 1)
                dve.wait_ge(s_xru, n + 1)
                for k in range(16):
                    slot = k % RING
                    dve.wait_ge(s_ld[slot], 16 * (2 * n + k // RING + 1))
                    stt(ring[:, slot, :], ring[:, slot, :], 1.0, XR[:, :], ALU.mult, ALU.mult,
                        accum_out=DOT[:, k:k + 1]).then_inc(s_dots, 1)
                    gaps(gap, l, i, j, k)
                    if k == ROUTE:
                        if not (number(n) and n < 2):
                            dve.wait_ge(s_vused, 16 * (n - 1))
                        dve.wait_ge(s_IDU, n + 1)
                        dve.tensor_copy(IDV[par][:, :], IDU[par][:, :]).then_inc(s_IDV, 1)
                        dve.wait_ge(s_IDV, n + 1)
                        if after(l, i, j):
                            route(*after(l, i, j), 1 - par)
                dve.wait_ge(s_gelu, n + 1)
                if not first:
                    dve.wait_ge(s_DG, 16 * n)
                tt(AV[:, :], GL[:, :], GA[par][:, :], ALU.mult).then_inc(s_act, 1)
                dve.wait_ge(s_act, n + 1)
                last = before(l, i, j)
                if last and ends(*last):
                    fin(*last)

            def fin(l, i, j):
                n = NT[i]
                dve.wait_ge(s_vused, 16 * (group_no(l, i, j) + 1))
                tt(hx[:n, i, :], hx[:n, i, :], bank[:n, 6:8, :].rearrange("p b n -> p (b n)"), ALU.add).then_inc(s_fin, 1)

            route(*GROUPS[0], 0)
            walk(dve, step, c, UP_STEPS)
            fin(*GROUPS[-1])

        @block.tensor
        def _(pe):
            mm = pe.matmul

            def put(dst, src):
                return pe.transpose(dst, src, ident[:src.shape[0], :src.shape[0]])

            pe.wait_ge(s_const, 1)
            pe.wait_ge(s_small, 96)
            put(bank[:, 0, 0:40], g_rows[:40, :])
            for m in range(4):
                put(bank[:, 1, P * m:P * m + P], sk_rows[:, m, :])
            mm(bank[:, 2, 0:240], XS[:GT, :], spread[:GT, :], start=True, stop=True).then_inc(s_tr, 1)

            def xht(kind, i):
                k, n = NORM[kind, i], NT[i]
                pe.wait_ge(s_xh, k + 1)
                for hf in range(2):
                    if k:
                        pe.wait_ge(s_xT, XTC[k - 1])
                    for m in range(4):
                        cc = 4 * hf + m
                        ins = put(bank[:, 4 + hf, m * n:m * n + n], XH[:n, P * cc:P * cc + P])
                    ins.then_inc(s_xhT, 1)

            def project(i, part):
                n, b = NT[i], PBANK[i, part]
                src = xT if i == 1 else xT2
                o = META if i else 0
                if part == "k" and i == 2:
                    pe.wait_ge(s_pj, PARTS[0, "k"])
                    pe.wait_ge(s_pjd, WITH_K[0, "k"])
                pe.wait_ge(s_xT, XTC[NORM["a", i]])
                cols = []
                if part != "k":
                    cols += [(0, 512), (512, 1024)]
                if part != "q":
                    cols += [(1024, 1536), (1536, A_COLS) if i else (1792, 1856)]
                for cc in range(KC):
                    if i == 1:
                        pe.wait_ge(s_win[cc], 32)
                        if cc in (2, 5):
                            xht("a", 0 if cc == 2 else 2)
                    for m, (a, z) in enumerate(cols):
                        w = w_q[:, cc, a:z] if a < Q_COLS else w_r[:, cc, a - Q_COLS:z - Q_COLS]
                        ins = mm(bank[:n, b + m, :z - a], src[:, cc, o:o + n], w, start=cc == 0, stop=cc == KC - 1)
                ins.then_inc(s_proj, 1)

            def qk_t(i, part):
                n, pj = NT[i], PJ[i, part]
                pe.wait_ge(s_roped, PARTS[i, part])
                if part != "k":
                    for h in range(8):
                        a = h * n
                        ins = put(bank[:, a // 512, a % 512:a % 512 + n], pj[:n, h, :])
                if part != "q":
                    for m, b in enumerate((8, 9, 12, 13, 14) if i else (8, 9, 14)):
                        a = m * n
                        ins = put(bank[:, KBANK[i] + a // 512, a % 512:a % 512 + n], pj[:n, b, :])
                ins.then_inc(s_qkT, 1)
                if part == "q":
                    pe.wait_ge(s_qk, WITH_Q[i, part])

            def select(i):
                n = NT[i]
                pe.wait_ge(s_qkd, WITH_K[i, "k"] if i == 2 else WITH_K[0, "k"])
                for h in range(IDX_HEADS):
                    r = slice(64 * (h % 2), 64 * (h % 2) + 64)
                    ins = mm(bank[:n, h, :KEYS[i]], qiT[i][r, h // 2, :], kiT[r, :KEYS[i]], start=True, stop=True)
                ins.then_inc(s_idx, 1)

            def logits(l, i, g):
                n, keys = NT[i], KEYS[i]
                if l == 1 and g == 0:
                    pe.wait_ge(s_ev, EV[first_block(1, i, "wo")])
                for h in range(GROUP):
                    ins = mm(logit_banks(l, i, g)[:, h, :], qT[i][:, GROUP * g + h, :], kT[:, g, :keys], start=True, stop=True)
                ins.then_inc(s_logit, 1)

            def turn(l, i, g):
                n, u = NT[i], 2 * ATT[l, i] + g
                if l == 0:
                    pe.wait_ge(s_prob, u + 1)
                else:
                    pe.wait_ge(s_probb, u - 6 + 1)
                for j in range(i + 1):
                    for h in range(GROUP):
                        ins = put(bank[:, turn_bank(l, i, g, j), h * n:h * n + n],
                                  logits_at(l, i, g)[:n, h, OFF[j]:OFF[j] + P])
                ins.then_inc(s_PTp, 1)

            def pv(l, i, g):
                n, u = NT[i], 2 * ATT[l, i] + g
                pe.wait_ge(s_PT, u + 1)
                if i:
                    pe.wait_ge(s_PTd, PTD[l, i] + g + 1)
                for j in range(i + 1):
                    kn = NT[j]
                    ins = mm(bank[:, pv_bank(l, i, g), :GROUP * n], V[:kn, j, P * g:P * g + P], weights_at(l, i, g)[:kn, j, :GROUP * n],
                             start=j == 0, stop=j == i)
                ins.then_inc(s_pv, 1)
                if (l, i, g) != (0, 1, 0):
                    pe.wait_ge(s_oT, u + 1)

            def weights(b):
                pe.wait_ge(s_wb[b % WB], 16 * (b // WB + 1))
                return wb[:, b % WB, :, :]

            def copies(b):
                e = EV[b]
                if e >= 3:
                    pe.wait_ge(s_ev, e - 2)
                return 3 + e % 3

            def wo(l, i, m):
                b = first_block(l, i, "wo") + m
                if (l, i) == (0, 2) and m == 4:
                    pe.wait_ge(s_res, WO_CHUNK[l, i] + 1)
                w = weights(b)
                d = slice(P * (m % 4), P * (m % 4) + P)
                for h in range(HEADS):
                    ins = mm(bank[:, 3 + 2 * (m // 4), d], oT[i][:, h, :], w[:, h, :], start=h == 0, stop=h == HEADS - 1)
                if (l, i) == (0, 2):
                    for h in range(HEADS):
                        ins = mm(bank[:META, 4, d], oT[0][:, h, :], w[:, h, :], start=h == 0, stop=h == HEADS - 1)
                ins.then_inc(s_wbu, 1)
                if m % 4 == 3:
                    pe.wait_ge(s_wbu, b + 1)
                    pe.sem_inc(s_wo, 1)

            def pq(l, i, m):
                o, w = (0, META + P) if (l, i) == (0, 2) else (META, P)
                if m == 0:
                    pe.wait_ge(s_xT, XTC[NORM[("f0", "f1")[l], i]])
                b = first_block(l, i, "pq") + m
                k, ws = copies(b), weights(b)
                for cc in range(KC):
                    ins = mm(bank[:, k, :w], ws[:, cc, :], xT[:, cc, o:o + w], start=cc == 0, stop=cc == KC - 1)
                ins.then_inc(s_wbu, 1)

            def kv(i, m):
                pe.wait_ge(s_xT, XTC[NORM["b", i]])
                o, w = (0, META + P) if i == 1 else (META, P)
                b = first_block(1, i, "kv") + m
                k, ws = copies(b), weights(b)
                if m < 2:
                    for cc in range(KC):
                        ins = mm(bank[:, k, :w], ws[:, cc, :], xT2[:, cc, o:o + w], start=cc == 0, stop=cc == KC - 1)
                else:
                    for cc in range(KC):
                        ins = mm(bank[:, k, :P], xT2[:, cc, META:META + P], ws[:, cc, :], start=cc == 0,
                                 stop=cc == KC - 1)
                    if i == 1:
                        for cc in range(KC):
                            ins = mm(bank[:META, k, P:2 * P], xT2[:, cc, 0:META], ws[:, cc, :], start=cc == 0,
                                     stop=cc == KC - 1)
                ins.then_inc(s_wbu, 1)

            def bq(i, m):
                b = first_block(1, i, "bq") + m
                k, ws = copies(b), weights(b)
                for cc in range(KC):
                    ins = mm(bank[:, k, :P], ws[:, cc, :], xT[:, cc, META:META + P], start=cc == 0, stop=cc == KC - 1)
                ins.then_inc(s_wbu, 1)

            gap = {"xhT": xht, "project": project, "qkT": qk_t, "logits": logits, "turn": turn, "pv": pv, "wo": wo,
                   "pq": pq, "kv": kv, "bq": bq}

            pe.wait_ge(s_setup, 1)
            xht("a", 1)
            project(1, "all")
            project(0, "k")
            qk_t(1, "all")
            pe.wait_ge(s_xT, XTC[2])
            qk_t(0, "k")
            pe.wait_ge(s_qk, 1)
            select(1)
            pe.wait_ge(s_relu, 1)
            for g in range(2):
                logits(0, 1, g)
            project(2, "k")
            for g in range(2):
                turn(0, 1, g)
            for g in range(2):
                pv(0, 1, g)
            for m in range(4):
                wo(0, 1, m)
            qk_t(2, "k")
            for m in range(4, 8):
                wo(0, 1, m)
            select(2)
            xht("f0", 1)
            pe.wait_ge(s_relu, 2)
            for m in range(16):
                pq(0, 1, m)

            def route(l, i, j):
                n = group_no(l, i, j)
                nt = NT[i]
                pe.wait_ge(s_XS, n + 1)
                if not (number(n) and n == 0):
                    pe.wait_ge(s_xru, n)
                for m in range(2):
                    ins = mm(bank[:, m, :], XS[:nt, :], hx[:nt, i, 512 * m:512 * m + 512], start=True, stop=True)
                ins.then_inc(s_xr, 1)
                pe.wait_ge(s_QG, n + 1)
                if not (number(n) and n == 0):
                    pe.wait_ge(s_S, n)
                for h in range(2):
                    ins = mm(bank[:, 2, P * h:P * h + P], QG[:, P * h:P * h + P], skT[:, 2 * l + h, :],
                             start=True, stop=True)
                ins.then_inc(s_s, 1)

            def clear(l, i):
                if (l, i) != ORDER[0]:
                    pe.wait_ge(s_fin, FIN[l, i] - 1)
                else:
                    pe.wait_ge(s_pj, PARTS[2, "q"])
                for m in range(2):
                    mm(bank[:, 6 + m, :].rearrange("p (a b) -> p a b", b=P), zeros[:, :],
                       zeros[:, :].unsqueeze(1).broadcast_to([P, 4, P]), start=True, stop=False,
                       skip_group_check=True)

            def v_sum(n, k):
                slot = RING + k % RING
                pe.wait_ge(s_DG, 16 * n + k + 1)
                pe.wait_ge(s_ld[slot], 16 * (2 * n + k // RING + 1))
                for m in range(2):
                    ins = mm(bank[:, 6 + m, :], DG[:, k, :], ring[:, slot, 512 * m:512 * m + 512],
                             start=False, stop=False, skip_group_check=True)
                ins.then_inc(s_vused, 1)

            def step(l, i, j, par):
                n = group_no(l, i, j)
                last = before(l, i, j)
                for k in range(16):
                    if last:
                        v_sum(n - 1, k)
                    if number(j) and any(s == k and name in IN_ROW_BANKS for s, name, *_ in work.get((l, i, j), ())):
                        pe.wait_ge(s_xru, n + 1)
                    gaps(gap, l, i, j, k)
                    if k == ROUTE and after(l, i, j):
                        route(*after(l, i, j))
                if not last or ends(*last):
                    clear(l, i)

            route(*GROUPS[0])
            walk(pe, step)
            for k in range(16):
                v_sum(len(GROUPS) - 1, k)


_INS = ["x", "meta_tokens", "a_norm", "a_w_in", "a_q_norm", "a_k_norm", "a_w_o", "kv_norm", "kv_w", "b_norm",
        "b_w_q", "b_w_o", "ffn_norm", "peer_w_q", "peer_subkeys", "peer_u", "peer_v"]


def _rope_table():
    import numpy as np
    pos = np.arange(T, dtype=np.float32)
    cols = []
    for r in (32, 16):
        inv = np.float32(500000.0) ** (-np.arange(r // 2, dtype=np.float32) * np.float32(2.0) / np.float32(r))
        ang = pos[:, None] * inv[None, :].astype(np.float32)
        cols += [np.cos(ang), np.sin(ang)]
    return np.ascontiguousarray(np.concatenate(cols, axis=1).astype(np.float32))


def kernel(**inputs):
    import numpy as _np
    import concourse.bacc as _bacc
    from concourse import mybir as _mybir
    from concourse.bass_utils import run_bass_kernel_spmd as _run

    nc = _bacc.Bacc("TRN2", target_bir_lowering=False, num_devices=1)
    arrays, args = {}, []
    for name in _INS + ["rope"]:
        a = _rope_table() if name == "rope" else _np.ascontiguousarray(inputs[name])
        arrays[f"in_{name}_dram"] = a
        args.append(nc.dram_tensor(f"in_{name}_dram", a.shape, _mybir.dt.from_np(a.dtype), kind="ExternalInput").ap())
    args.append(nc.dram_tensor("out_0_dram", (1, 2 * P, D), F32, kind="ExternalOutput").ap())
    build(nc, *args)
    r = _run(nc, [arrays], core_ids=[0])
    return r.results[0]["out_0_dram"]
```
